# Optimizing a Trainium2 kernel written in Bass

```python
import jax, jax.numpy as jnp
from jax import lax
import numpy as np

D_MODEL = 1024
BATCH = 1
SEQ = 1024
DEPTH = 2
DEC_BATCH = 8
DEC_SEQ = 1
PAST_LEN = 2048
PAGE_SIZE = 128

N_MIXERS = 4
MIXER_STICK = 0
MIXER_FOX = 1
MIXER_MOBA = 2
MIXER_DSA = 3
N_HEADS = 16
N_KV_HEADS = 4
HEAD_DIM = D_MODEL // N_HEADS
KV_GROUP = N_HEADS // N_KV_HEADS
D_FF = 2816
CONV_WIDTH = 3
ROPE_THETA = 10000.0
RMS_EPS = 1e-6
Q_BLOCK = 128
MOBA_BLOCK = 256
MOBA_TOPK = 3
MOBA_Q_CHUNK = 16
IDX_HEADS = 8
IDX_DIM = 64
IDX_TOPK_MAX = 256
FORGET_BIAS_INIT = 3.0

kernel_name = "hybrid_stickbreak_fox_moba_dsa_step"

def rms_norm(x, g):
    xf = x.astype(jnp.float32)
    y = xf * lax.rsqrt(jnp.mean(xf * xf, axis=-1, keepdims=True) + RMS_EPS)
    return (y * g.astype(jnp.float32)).astype(x.dtype)

def rotary(x, pos):
    d = x.shape[-1]
    half = d // 2
    inv_freq = jnp.power(ROPE_THETA, -jnp.arange(half, dtype=jnp.float32) * (2.0 / d))
    ang = pos.astype(jnp.float32)[:, None] * inv_freq[None, :]
    cos = jnp.cos(ang)[None, :, None, :]
    sin = jnp.sin(ang)[None, :, None, :]
    xf = x.astype(jnp.float32)
    x1, x2 = xf[..., :half], xf[..., half:]
    return jnp.concatenate([x1 * cos - x2 * sin, x2 * cos + x1 * sin], axis=-1).astype(x.dtype)

def split_qkv(qkv, B, T):
    nq = N_HEADS * HEAD_DIM
    nk = N_KV_HEADS * HEAD_DIM
    q = qkv[..., :nq].reshape(B, T, N_HEADS, HEAD_DIM)
    k = qkv[..., nq:nq + nk].reshape(B, T, N_KV_HEADS, HEAD_DIM)
    v = qkv[..., nq + nk:].reshape(B, T, N_KV_HEADS, HEAD_DIM)
    return q, k, v

def gather_pages(pool, page_table):
    rows = pool[page_table]
    db, n_pages, page = rows.shape[:3]
    return rows.reshape((db, n_pages * page) + rows.shape[3:])

def extend_with_past(new, pool, page_table):
    if page_table is None:
        return new
    return jnp.concatenate([gather_pages(pool, page_table).astype(new.dtype), new], axis=1)

def sweep_queries(fn, q_arrays, q_off, block):
    tq = q_arrays[0].shape[1]
    blk = block if tq % block == 0 else tq
    nb = tq // blk
    pos = (q_off + jnp.arange(tq, dtype=jnp.int32)).reshape(nb, blk)
    split = tuple(jnp.moveaxis(a.reshape((a.shape[0], nb, blk) + a.shape[2:]), 1, 0) for a in q_arrays)
    out = lax.map(lambda args: fn(args[0], *args[1]), (pos, split))
    out = jnp.moveaxis(out, 0, 1)
    return out.reshape((out.shape[0], tq) + out.shape[3:])

def stick_breaking_attention(q, k, v, q_off):
    B, _, H, Dh = q.shape
    L = k.shape[1]
    key_pos = jnp.arange(L, dtype=jnp.int32)
    scale = Dh ** -0.5

    def block(pos, qb):
        Q = qb.shape[1]
        qg = qb.reshape(B, Q, N_KV_HEADS, KV_GROUP, Dh)
        z = jnp.einsum('bqngd,bsnd->bngqs', qg, k, preferred_element_type=jnp.float32) * scale
        past = key_pos[None, :] < pos[:, None]
        log_keep = jnp.where(past, jax.nn.log_sigmoid(-z), 0.0)
        log_between = lax.cumsum(log_keep, axis=z.ndim - 1, reverse=True) - log_keep
        w = jnp.where(past, jnp.exp(jax.nn.log_sigmoid(z) + log_between), 0.0)
        o = jnp.einsum('bngqs,bsnd->bqngd', w.astype(v.dtype), v)
        return o.reshape(B, Q, H, Dh)

    return sweep_queries(block, (q,), q_off, Q_BLOCK)

def forgetting_attention(q, k, v, log_f, q_off):
    B, _, H, Dh = q.shape
    L = k.shape[1]
    key_pos = jnp.arange(L, dtype=jnp.int32)
    scale = Dh ** -0.5
    cum = lax.cumsum(log_f.astype(jnp.float32), axis=1)
    cum = jnp.transpose(cum, (0, 2, 1)).reshape(B, N_KV_HEADS, KV_GROUP, L)

    def block(pos, qb):
        Q = qb.shape[1]
        qg = qb.reshape(B, Q, N_KV_HEADS, KV_GROUP, Dh)
        z = jnp.einsum('bqngd,bsnd->bngqs', qg, k, preferred_element_type=jnp.float32) * scale
        decay = cum[..., pos][..., None] - cum[..., None, :]
        visible = key_pos[None, :] <= pos[:, None]
        p = jax.nn.softmax(jnp.where(visible, z + decay, -jnp.inf), axis=-1)
        o = jnp.einsum('bngqs,bsnd->bqngd', p.astype(v.dtype), v)
        return o.reshape(B, Q, H, Dh)

    return sweep_queries(block, (q,), q_off, Q_BLOCK)

def moba_attention(q, k, v, q_off):
    B, _, H, Dh = q.shape
    L = k.shape[1]
    nb = -(-L // MOBA_BLOCK)
    pad = nb * MOBA_BLOCK - L
    scale = Dh ** -0.5

    def to_blocks(a):
        a = jnp.pad(a, ((0, 0), (0, pad), (0, 0), (0, 0)))
        return a.reshape(B, nb, MOBA_BLOCK, N_KV_HEADS, Dh).transpose(0, 3, 1, 2, 4)

    kb, vb = to_blocks(k), to_blocks(v)
    kv_head = jnp.arange(H) // KV_GROUP
    k_mean = jnp.mean(kb.astype(jnp.float32), axis=3)[:, kv_head]
    n_sel = min(MOBA_TOPK, nb)
    bidx = jnp.arange(B)[:, None, None, None]
    hidx = kv_head[None, :, None, None]
    in_block = jnp.arange(MOBA_BLOCK, dtype=jnp.int32)
    blk_ids = jnp.arange(nb, dtype=jnp.int32)

    def block(pos, qb):
        Q = qb.shape[1]
        qh = jnp.transpose(qb, (0, 2, 1, 3))
        own = pos // MOBA_BLOCK
        gate = jnp.einsum('bhqd,bhnd->bhqn', qh.astype(jnp.float32), k_mean)
        gate = jnp.where(blk_ids[None, :] < own[:, None], gate, -jnp.inf)
        _, sel = lax.top_k(gate, n_sel)
        sel = sel.astype(jnp.int32)
        own_b = jnp.broadcast_to(own[None, None, :, None], (B, H, Q, 1))
        chosen = jnp.concatenate([sel, own_b], axis=-1)
        chosen_ok = jnp.concatenate([sel < own[None, None, :, None], jnp.ones((B, H, Q, 1), dtype=bool)], axis=-1)
        kg = kb[bidx, hidx, chosen]
        vg = vb[bidx, hidx, chosen]
        s = jnp.einsum('bhqd,bhqnmd->bhqnm', qh, kg, preferred_element_type=jnp.float32) * scale
        key_pos = chosen[..., None] * MOBA_BLOCK + in_block
        ok = chosen_ok[..., None] & (key_pos <= pos[None, None, :, None, None])
        s = jnp.where(ok, s, -jnp.inf)
        ns = chosen.shape[-1]
        p = jax.nn.softmax(s.reshape(B, H, Q, ns * MOBA_BLOCK), axis=-1).reshape(s.shape)
        return jnp.einsum('bhqnm,bhqnmd->bqhd', p.astype(v.dtype), vg)

    return sweep_queries(block, (q,), q_off, MOBA_Q_CHUNK)

def dsa_attention(q, q_idx, w_idx, k, v, k_idx, q_off):
    B, _, H, Dh = q.shape
    L = k.shape[1]
    n_keep = min(IDX_TOPK_MAX, L // 4)
    key_pos = jnp.arange(L, dtype=jnp.int32)
    bidx = jnp.arange(B)[:, None, None]
    scale = Dh ** -0.5

    def block(pos, qb, qib, wib):
        Q = qb.shape[1]
        dots = jnp.einsum('bqid,bsd->bqis', qib, k_idx, preferred_element_type=jnp.float32)
        score = jnp.einsum('bqi,bqis->bqs', wib.astype(jnp.float32), jax.nn.relu(dots))
        score = jnp.where(key_pos[None, None, :] <= pos[None, :, None], score, -jnp.inf)
        _, sel = lax.top_k(score, n_keep)
        sel_ok = sel <= pos[None, :, None]
        kg = k[bidx, sel]
        vg = v[bidx, sel]
        qg = qb.reshape(B, Q, N_KV_HEADS, KV_GROUP, Dh)
        s = jnp.einsum('bqngd,bqknd->bqngk', qg, kg, preferred_element_type=jnp.float32) * scale
        p = jax.nn.softmax(jnp.where(sel_ok[:, :, None, None, :], s, -jnp.inf), axis=-1)
        o = jnp.einsum('bqngk,bqknd->bqngd', p.astype(v.dtype), vg)
        return o.reshape(B, Q, H, Dh)

    return sweep_queries(block, (q, q_idx, w_idx), q_off, Q_BLOCK)

def conv_ffn(h, prev, w_a, w_b, conv_w, conv_b, w_down):
    a = h @ w_a
    g = h @ w_b
    a_ext = jnp.concatenate([prev.astype(a.dtype), a], axis=1)
    T = a.shape[1]
    conv = conv_b + sum(conv_w[j] * a_ext[:, j:j + T] for j in range(CONV_WIDTH))
    y = (jax.nn.gelu(conv) * g) @ w_down
    return y, a_ext[:, -(CONV_WIDTH - 1):]

def decoder_trunk(x, q_off, cache_k, cache_v, cache_logf, cache_kidx, state_conv, page_table,
                  norm_mix, norm_ffn, norm_final, w_qkv, w_o, fox_w_f, fox_b_f,
                  idx_w_q, idx_w_k, idx_w_w, ffn_w_a, ffn_w_b, ffn_conv_w, ffn_conv_b, ffn_w_down):
    B, T, _ = x.shape
    decoding = page_table is not None
    pos = q_off + jnp.arange(T, dtype=jnp.int32)
    new_k, new_v, new_conv = [], [], []
    new_logf = None
    new_kidx = None
    for i in range(DEPTH):
        kind = i % N_MIXERS
        h = rms_norm(x, norm_mix[i])
        q, k, v = split_qkv(h @ w_qkv[i], B, T)
        if kind in (MIXER_MOBA, MIXER_DSA):
            q = rotary(q, pos)
            k = rotary(k, pos)
        new_k.append(k)
        new_v.append(v)
        k_all = extend_with_past(k, cache_k[i] if decoding else None, page_table)
        v_all = extend_with_past(v, cache_v[i] if decoding else None, page_table)
        if kind == MIXER_STICK:
            o = stick_breaking_attention(q, k_all, v_all, q_off)
        elif kind == MIXER_FOX:
            logf = jax.nn.log_sigmoid((h @ fox_w_f + fox_b_f).astype(jnp.float32))
            new_logf = logf
            o = forgetting_attention(q, k_all, v_all, extend_with_past(logf, cache_logf, page_table), q_off)
        elif kind == MIXER_MOBA:
            o = moba_attention(q, k_all, v_all, q_off)
        else:
            qi = rotary((h @ idx_w_q).reshape(B, T, IDX_HEADS, IDX_DIM), pos)
            ki = rotary((h @ idx_w_k).reshape(B, T, 1, IDX_DIM), pos)[:, :, 0]
            wi = (h @ idx_w_w) * (IDX_HEADS ** -0.5 * IDX_DIM ** -0.5)
            new_kidx = ki
            o = dsa_attention(q, qi, wi, k_all, v_all, extend_with_past(ki, cache_kidx, page_table), q_off)
        x = x + o.reshape(B, T, D_MODEL) @ w_o[i]
        h = rms_norm(x, norm_ffn[i])
        prev = state_conv[i] if decoding else jnp.zeros((B, CONV_WIDTH - 1, D_FF), x.dtype)
        y, conv_rows = conv_ffn(h, prev, ffn_w_a[i], ffn_w_b[i], ffn_conv_w[i], ffn_conv_b[i], ffn_w_down[i])
        new_conv.append(conv_rows)
        x = x + y
    return (rms_norm(x, norm_final), jnp.stack(new_k), jnp.stack(new_v), new_logf, new_kidx, jnp.stack(new_conv))

def setup_inputs(seed: int = 0) -> dict:
    key = jax.random.key(seed)
    ks = jax.random.split(key, 24)
    f32 = jnp.float32
    n_pages = PAST_LEN // PAGE_SIZE
    n_used = DEC_BATCH * n_pages
    n_pool = n_used + max(1, n_used // 4)
    qkv_cols = (N_HEADS + 2 * N_KV_HEADS) * HEAD_DIM

    def nrm(k, shape, scale=1.0):
        return jax.random.normal(k, shape, f32) * scale

    x_prompt = nrm(ks[0], (BATCH, SEQ, D_MODEL))
    x_sample = nrm(ks[1], (DEC_BATCH, DEC_SEQ, D_MODEL))
    cache_k = nrm(ks[2], (DEPTH, n_pool, PAGE_SIZE, N_KV_HEADS, HEAD_DIM))
    cache_v = nrm(ks[3], (DEPTH, n_pool, PAGE_SIZE, N_KV_HEADS, HEAD_DIM))
    cache_logf = jax.nn.log_sigmoid(FORGET_BIAS_INIT + nrm(ks[4], (n_pool, PAGE_SIZE, N_HEADS)))
    cache_kidx = nrm(ks[5], (n_pool, PAGE_SIZE, IDX_DIM))
    state_conv = nrm(ks[6], (DEPTH, DEC_BATCH, CONV_WIDTH - 1, D_FF))
    page_table = jax.random.permutation(ks[7], n_pool)[:n_used].reshape(DEC_BATCH, n_pages).astype(jnp.int32)

    norm_mix = 1.0 + nrm(ks[8], (DEPTH, D_MODEL), 0.01)
    norm_ffn = 1.0 + nrm(ks[9], (DEPTH, D_MODEL), 0.01)
    norm_final = 1.0 + nrm(ks[10], (D_MODEL,), 0.01)
    w_qkv = nrm(ks[11], (DEPTH, D_MODEL, qkv_cols), D_MODEL ** -0.5)
    w_o = nrm(ks[12], (DEPTH, D_MODEL, D_MODEL), D_MODEL ** -0.5)
    fox_w_f = nrm(ks[13], (D_MODEL, N_HEADS), D_MODEL ** -0.5)
    fox_b_f = FORGET_BIAS_INIT + nrm(ks[14], (N_HEADS,), 0.1)
    idx_w_q = nrm(ks[15], (D_MODEL, IDX_HEADS * IDX_DIM), D_MODEL ** -0.5)
    idx_w_k = nrm(ks[16], (D_MODEL, IDX_DIM), D_MODEL ** -0.5)
    idx_w_w = nrm(ks[17], (D_MODEL, IDX_HEADS), D_MODEL ** -0.5)
    ffn_w_a = nrm(ks[18], (DEPTH, D_MODEL, D_FF), D_MODEL ** -0.5)
    ffn_w_b = nrm(ks[19], (DEPTH, D_MODEL, D_FF), D_MODEL ** -0.5)
    ffn_conv_w = nrm(ks[20], (DEPTH, CONV_WIDTH, D_FF), CONV_WIDTH ** -0.5)
    ffn_conv_b = nrm(ks[21], (DEPTH, D_FF), 0.01)
    ffn_w_down = nrm(ks[22], (DEPTH, D_FF, D_MODEL), D_FF ** -0.5)
    return {"x_prompt": x_prompt, "x_sample": x_sample, "cache_k": cache_k, "cache_v": cache_v,
            "cache_logf": cache_logf, "cache_kidx": cache_kidx, "state_conv": state_conv,
            "page_table": page_table, "norm_mix": norm_mix, "norm_ffn": norm_ffn, "norm_final": norm_final,
            "w_qkv": w_qkv, "w_o": w_o, "fox_w_f": fox_w_f, "fox_b_f": fox_b_f, "idx_w_q": idx_w_q,
            "idx_w_k": idx_w_k, "idx_w_w": idx_w_w, "ffn_w_a": ffn_w_a, "ffn_w_b": ffn_w_b,
            "ffn_conv_w": ffn_conv_w, "ffn_conv_b": ffn_conv_b, "ffn_w_down": ffn_w_down}

def reference(x_prompt, x_sample, cache_k, cache_v, cache_logf, cache_kidx, state_conv, page_table,
              norm_mix, norm_ffn, norm_final, w_qkv, w_o, fox_w_f, fox_b_f, idx_w_q, idx_w_k, idx_w_w,
              ffn_w_a, ffn_w_b, ffn_conv_w, ffn_conv_b, ffn_w_down):
    weights = (norm_mix, norm_ffn, norm_final, w_qkv, w_o, fox_w_f, fox_b_f, idx_w_q, idx_w_k, idx_w_w,
               ffn_w_a, ffn_w_b, ffn_conv_w, ffn_conv_b, ffn_w_down)
    y_prompt, k_p, v_p, logf_p, kidx_p, conv_p = decoder_trunk(
        x_prompt, 0, None, None, None, None, None, None, *weights)
    past_len = page_table.shape[1] * cache_k.shape[2]
    y_sample, k_s, v_s, logf_s, kidx_s, conv_s = decoder_trunk(
        x_sample, past_len, cache_k, cache_v, cache_logf, cache_kidx, state_conv, page_table, *weights)
    return (y_prompt, y_sample, k_p, v_p, k_s, v_s, logf_p, logf_s, kidx_p, kidx_s, conv_p, conv_s)


_drawn_inputs = setup_inputs


def setup_inputs(seed=0):
    import zlib

    import numpy as np

    out = dict(_drawn_inputs(seed))
    spreads = {}
    factors = {'norm_mix': 5.089,
     'norm_ffn': 5.028,
     'norm_final': 33.791,
     'ffn_conv_b': 8.0,
     'cache_logf': 4.772}
    for name, (base, spread) in spreads.items():
        noise = np.random.default_rng([zlib.crc32(name.encode()), seed]).standard_normal(out[name].shape)
        drawn = base * np.exp(spread * noise) if base else spread * noise
        out[name] = __import__('jax').numpy.asarray(drawn.astype(out[name].dtype))
    for name, factor in factors.items():
        out[name] = (out[name] * factor).astype(out[name].dtype)
    return out
```

```python
import concourse.bass as bass
from concourse import mybir
from contextlib import ExitStack, contextmanager

F32 = mybir.dt.float32
F32R = mybir.dt.float32r
I32 = mybir.dt.int32
ALU = mybir.AluOpType
ACT = mybir.ActivationFunctionType
AX = mybir.AxisListType
P = 128
HALF = 64
GROUP_COLS = 256
NEG = -1.0e30
RMS_EPS = 1e-6
EXP_LN_SET = "natural_log_exp_and_others"


def trunk_program(nc, x_prompt, x_sample, cache_k, cache_v, cache_logf, state_conv, page_table,
                  norm_mix, norm_ffn, norm_final, w_qkv, w_o, fox_w_f, fox_b_f,
                  ffn_w_a, ffn_w_b, ffn_conv_w, ffn_conv_b, ffn_w_down,
                  y_prompt, y_sample, k_prompt, v_prompt, k_sample, v_sample,
                  logf_prompt, logf_sample, conv_prompt, conv_sample):
    SEQ, D = x_prompt.shape[1], x_prompt.shape[2]
    NB = x_sample.shape[0]
    DEPTH, POOL, PAGE, NKV, DH = cache_k.shape
    NPAGE = page_table.shape[1]
    NH = D // DH
    HG = NH // NKV
    KVD = NKV * DH
    F = ffn_w_a.shape[2]
    TOK = SEQ + NB
    KT = D // P
    ST = SEQ // P
    CG = 3
    NG = TOK // CG
    FT = F // P
    CHUNKS = F // GROUP_COLS
    NPAR = 2 * NB + 4
    SCALE = float(DH) ** -0.5
    assert TOK % (2 * CG) == 0 and NG <= 512 and DH == HALF and PAGE == P and NKV == 4 and HG == 4
    assert F % GROUP_COLS == 0 and SEQ % P == 0

    ctx = ExitStack()
    with ctx:
        base = ctx.enter_context(nc.sbuf_tensor("arena", [P, (nc.sbuf_usable_end - nc.sbuf_base - 256) // 4], F32))
        start = nc.sbuf_base - 4 * base.shape[1]
        start += -start % 32
        room = 4 * base.shape[1] - 32
        TILE = TOK * 4
        KTILES = KT * TILE
        RAW = KT * GROUP_COLS * 4
        X, A, B, C = start, start + KTILES, start + 2 * KTILES, start + 3 * KTILES
        W = start + 4 * KTILES
        WBYTES = 7 * RAW
        DD = W + WBYTES
        CONST = DD + 4 * TILE

        def at(name, shape, off, dt=F32):
            return nc.alloc_sbuf_tensor_at(name, shape, dt, offset=off)

        pos = [CONST]

        def const(name, shape, dt=F32):
            n = 4
            for s in shape[1:]:
                n *= s
            off = pos[0]
            pos[0] += n + (-n % 32)
            assert pos[0] <= start + room, (name, pos[0] - start, room)
            return at(name, shape, off, dt)

        ident = const("ident", [P, P])
        tri_incl = const("tri_incl", [P, P])
        tri_comp = const("tri_comp", [P, P])
        tri_strict = const("tri_strict", [P, P])
        ones = const("ones", [P, P])
        causal = const("causal", [P, P])
        gain = const("gain", [P, KT, 5])
        fpar = const("fpar", [P, FT, NPAR])
        fcur = const("fcur", [P, 2, NPAR])
        xT = at("xT", [P, KT, TOK], X)
        h_hi = at("h_hi", [P, KT, TOK], A, F32R)
        h_lo = at("h_lo", [P, KT, TOK], B, F32R)
        raw = at("raw", [P, KT, GROUP_COLS], W)
        w_hi = [at(f"w_hi{s}", [P, KT, GROUP_COLS], W + RAW * (1 + 2 * s), F32R) for s in range(3)]
        w_lo = [at(f"w_lo{s}", [P, KT, GROUP_COLS], W + RAW * (2 + 2 * s), F32R) for s in range(3)]
        qT = at("qT", [P, KT, TOK], C)
        kvT = at("kvT", [P, 4, TOK], DD)
        oT = at("oT", [P, KT, TOK], A)
        o_hi = at("o_hi", [P, KT, TOK], B, F32R)
        o_lo = at("o_lo", [P, KT, TOK], C, F32R)

        psum = ctx.enter_context(nc.psum_tensor("psum", [P, 8, 512], F32))
        acc = [psum[:, 3 * s:3 * s + 3, :] for s in range(2)]
        bank = [psum[:, 6 + b, :] for b in range(2)]

        def flat(b0, b1):
            return psum[:, b0:b1, :].rearrange("p b n -> p (b n)")

        ncum_dram = nc.dram_tensor("ncum_scratch", [NH, SEQ], F32, kind="Internal").ap()

        mine, before = [], []

        def sem(name):
            guard = nc.semaphore(name)
            mine.append((guard, guard.__enter__()))
            return mine[-1][1]

        @contextmanager
        def phase():
            with nc.Block() as block:
                @block.sync
                def _(sp):
                    for _, s in before:
                        sp.sem_clear(s)
                yield block
            for guard, _ in before:
                guard.__exit__(None, None, None)
            before[:] = mine
            mine.clear()

        def row(ap1d):
            return ap1d.rearrange("(a n) -> a n", a=1)

        def setup():
            xrow = at("xrow", [P, ST, D], A)
            xs_row = at("xs_row", [NB, D], B)
            nrow = at("nrow", [5, D], B + D * 4)
            loaded = sem("setup_loaded")
            s_id0, s_id = sem("setup_memset"), sem("setup_const")
            s_t, s_e, s_g = sem("setup_transposed"), sem("setup_evacuated"), sem("setup_gain")
            with phase() as block:
                @block.sync
                def _(sp):
                    for i in range(ST):
                        sp.dma_start(xrow[:, i, :], x_prompt[0, i * P:(i + 1) * P, :]).then_inc(loaded, 16)
                    sp.dma_start(xs_row[:, :], x_sample[:, 0, :]).then_inc(loaded, 16)
                    for n, r in enumerate((norm_mix[0], norm_mix[1], norm_ffn[0], norm_ffn[1], norm_final)):
                        sp.dma_start(nrow[n:n + 1, :], row(r)).then_inc(loaded, 16)

                @block.gpsimd
                def _(pool):
                    for t, v in ((ident, 0.0), (tri_incl, 1.0), (tri_comp, 1.0), (tri_strict, 1.0),
                                 (ones, 1.0), (causal, 0.0)):
                        nc.gpsimd.memset(t[:, :], v).then_inc(s_id0, 1)
                    pool.wait_ge(s_id0, 6)
                    for t, op, fill, b0, step, mul in (
                            (ident, ALU.not_equal, 1.0, 0, -1, 1),
                            (tri_incl, ALU.is_ge, 0.0, 0, -1, 1),
                            (tri_comp, ALU.is_ge, 0.0, -1, 1, -1),
                            (tri_strict, ALU.is_ge, 0.0, -1, -1, 1),
                            (causal, ALU.is_ge, NEG, 0, -1, 1)):
                        nc.gpsimd.affine_select(out=t[:, :], in_=t[:, :], compare_op=op, fill=fill, base=b0,
                                                pattern=[[step, P]], channel_multiplier=mul).then_inc(s_id, 1)

                @block.tensor
                def _(pe):
                    pe.wait_ge(s_id, 5)
                    pe.wait_ge(loaded, 16 * (ST + 6))
                    for c in range(KT):
                        if c >= 2:
                            pe.wait_ge(s_e, c - 1)
                        for i in range(ST):
                            nc.tensor.transpose(acc[c % 2][:, i // 4, (i % 4) * P:(i % 4 + 1) * P],
                                                xrow[:, i, c * P:(c + 1) * P], ident[:, :])
                        nc.tensor.transpose(acc[c % 2][:, 2, 0:NB], xs_row[:, c * P:(c + 1) * P],
                                            ident[0:NB, 0:NB])
                        nc.tensor.transpose(acc[c % 2][:, 2, 64:69], nrow[:, c * P:(c + 1) * P],
                                            ident[0:5, 0:5]).then_inc(s_t, 1)

                @block.vector
                def _(dve):
                    for c in range(KT):
                        dve.wait_ge(s_t, c + 1)
                        for b0 in range(0, ST, 4):
                            n = min(4, ST - b0) * P
                            nc.vector.tensor_copy(xT[:, c, b0 * P:b0 * P + n], acc[c % 2][:, b0 // 4, 0:n])
                        nc.vector.tensor_copy(gain[:, c, :], acc[c % 2][:, 2, 64:69])
                        nc.vector.tensor_copy(xT[:, c, SEQ:TOK], acc[c % 2][:, 2, 0:NB]).then_inc(s_e, 1)

        def norm(tag, g, final=False):
            sq = [at(f"sq{s}_{tag}", [P, TOK], W + s * TILE) for s in range(2)]
            var = at(f"var_{tag}", [P, TOK], W + 2 * TILE)
            rstd = at(f"rstd_{tag}", [P, TOK], W + 3 * TILE)
            full = [at(f"full{s}_{tag}", [P, TOK], W + (4 + s) * TILE) for s in range(2)]
            s_sq, s_mm, s_var = sem(f"sq_{tag}"), sem(f"sum_{tag}"), sem(f"var_{tag}")
            s_std, s_r, s_full, s_hi, s_lo = (sem(f"{n}_{tag}") for n in ("std", "rstd", "full", "hi", "lo"))
            with phase() as block:
                @block.scalar
                def _(act):
                    for k in range(KT):
                        if k >= 2:
                            act.wait_ge(s_mm, k - 1)
                        nc.scalar.activation(sq[k % 2][:, :], xT[:, k, :], ACT.Square).then_inc(s_sq, 1)
                    act.wait_ge(s_var, 1)
                    nc.scalar.activation(rstd[:, :], var[:, :], ACT.Sqrt).then_inc(s_std, 1)
                    if final:
                        return
                    for k in range(KT):
                        act.wait_ge(s_full, k + 1)
                        nc.scalar.activation(h_hi[:, k, :], full[k % 2][:, :], ACT.Copy).then_inc(s_hi, 1)

                @block.tensor
                def _(pe):
                    for k in range(KT):
                        pe.wait_ge(s_sq, k + 1)
                        for c in range(CG):
                            last = nc.tensor.matmul(acc[0][:, c, 0:NG], ones[:, :], sq[k % 2][:, c * NG:(c + 1) * NG],
                                                    start=(k == 0), stop=(k == KT - 1))
                        last.then_inc(s_mm, 1)

                @block.vector
                def _(dve):
                    dve.wait_ge(s_mm, KT)
                    nc.vector.tensor_scalar(var[:, :].rearrange("p (c n) -> p c n", c=CG), acc[0][:, :, 0:NG],
                                            1.0 / D, RMS_EPS, ALU.mult, ALU.add).then_inc(s_var, 1)
                    dve.wait_ge(s_std, 1)
                    nc.vector.reciprocal(rstd[:, :], rstd[:, :]).then_inc(s_r, 1)
                    dve.wait_ge(s_r, 1)
                    for k in range(KT):
                        if k >= 2 and not final:
                            dve.wait_ge(s_lo, k - 1)
                        out = xT[:, k, :] if final else full[k % 2][:, :]
                        nc.vector.scalar_tensor_tensor(out=out, in0=xT[:, k, :], scalar=gain[:, k, g:g + 1],
                                                       in1=rstd[:, :], op0=ALU.mult, op1=ALU.mult).then_inc(s_full, 1)

                @block.gpsimd
                def _(pool):
                    if final:
                        return
                    for k in range(KT):
                        pool.wait_ge(s_hi, k + 1)
                        nc.gpsimd.tensor_tensor(h_lo[:, k, :], full[k % 2][:, :], h_hi[:, k, :].bitcast(F32),
                                                ALU.subtract).then_inc(s_lo, 1)

        def split_product(out, hi, lo, cols, rhs_hi, rhs_lo, kt):
            for k in range(kt):
                for part, (w, r) in enumerate(((hi, rhs_hi), (hi, rhs_lo), (lo, rhs_hi))):
                    for c in range(CG):
                        last = nc.tensor.matmul(out[:, c, 0:NG], w[:, k, cols], r[:, k, c * NG:(c + 1) * NG],
                                                start=(k == 0 and part == 0), stop=(k == kt - 1 and part == 2))
            return last

        def gemm(tag, turns, weights, rhs_hi, rhs_lo, evacuate, source=None):
            s_w, s_hi, s_lo = sem(f"w_loaded_{tag}"), sem(f"w_hi_{tag}"), sem(f"w_lo_{tag}")
            s_slot, s_acc, s_free = sem(f"slot_used_{tag}"), sem(f"acc_ready_{tag}"), sem(f"acc_free_{tag}")
            s_rhi, s_rlo = sem(f"rhs_hi_{tag}"), sem(f"rhs_lo_{tag}")
            with phase() as block:
                @block.sync
                def _(sp):
                    with sp.Fori(0, turns) as i:
                        for u in range(2):
                            sp.wait_ge(s_lo, 2 * i + u + 1)
                            sp.dma_start(raw[:, :, :], weights(i, u)).then_inc(s_w, 16)

                @block.scalar
                def _(act):
                    if source is not None:
                        for k in range(KT):
                            nc.scalar.activation(rhs_hi[:, k, :], source[:, k, :], ACT.Copy).then_inc(s_rhi, 1)
                    with act.Fori(0, turns) as i:
                        for u in range(2):
                            act.wait_ge(s_w, 32 * i + 16 * (u + 1))
                            act.wait_ge(s_slot, 2 * i + u + 1)
                            nc.scalar.activation(w_hi[u][:, :, :], raw[:, :, :], ACT.Copy).then_inc(s_hi, 1)

                @block.gpsimd
                def _(pool):
                    pool.sem_inc(s_lo, 1)
                    with pool.Fori(0, turns) as i:
                        for u in range(2):
                            pool.wait_ge(s_hi, 2 * i + u + 1)
                            nc.gpsimd.tensor_tensor(w_lo[u][:, :, :], raw[:, :, :], w_hi[u][:, :, :].bitcast(F32),
                                                    ALU.subtract).then_inc(s_lo, 1)

                @block.tensor
                def _(pe):
                    pe.sem_inc(s_slot, 2)
                    if source is not None:
                        pe.wait_ge(s_rlo, KT)
                    with pe.Fori(0, turns) as i:
                        for u in range(2):
                            pe.wait_ge(s_lo, 2 * i + u + 2)
                            for m in range(2):
                                pe.wait_ge(s_free, 4 * i + 2 * u + m + 1)
                                split_product(acc[m], w_hi[u], w_lo[u], slice(m * P, (m + 1) * P),
                                              rhs_hi, rhs_lo, KT).then_inc(s_acc, 1)
                            pe.wait_ge(s_acc, 4 * i + 2 * u + 2)
                            pe.sem_inc(s_slot, 1)

                @block.vector
                def _(dve):
                    if source is not None:
                        for k in range(KT):
                            dve.wait_ge(s_rhi, k + 1)
                            nc.vector.tensor_tensor(rhs_lo[:, k, :], source[:, k, :], rhs_hi[:, k, :].bitcast(F32),
                                                    ALU.subtract).then_inc(s_rlo, 1)
                    dve.sem_inc(s_free, 2)
                    with dve.Fori(0, turns) as i:
                        for tile in range(4):
                            dve.wait_ge(s_acc, 4 * i + tile + 1)
                            evacuate(i, tile).then_inc(s_free, 1)

        def cols3(ap):
            return ap.rearrange("p a (c n) -> p (a c) n", c=CG)

        def project_qkv(l):
            view = w_qkv[l].rearrange("(k p) (t u n) -> p k t u n", p=P, u=2, n=GROUP_COLS)

            def group(turn0):
                return lambda i, u: view[:, :, bass.ds(i + turn0, 1), u, :].rearrange("p k t n -> p k (t n)")

            gemm(f"q{l}", D // (2 * GROUP_COLS), group(0), h_hi, h_lo,
                 lambda i, tile: nc.vector.tensor_scalar(cols3(qT[:, bass.ds(4 * i + tile, 1), :]),
                                                         acc[tile % 2][:, :, 0:NG], SCALE, None, ALU.mult))
            gemm(f"kv{l}", 1, group(D // (2 * GROUP_COLS)), h_hi, h_lo,
                 lambda i, tile: nc.vector.tensor_copy(cols3(kvT[:, tile:tile + 1, :]), acc[tile % 2][:, :, 0:NG]))

        tokm = at("tokm", [P, ST + 1, 2 * KVD], W)

        def kv_rows(l):
            s_t, s_e, s_out = sem(f"kv_turned_{l}"), sem(f"kv_rows_{l}"), sem(f"kv_stored_{l}")
            with phase() as block:
                @block.tensor
                def _(pe):
                    for i in range(ST + 1):
                        n = P if i < ST else NB
                        if i >= 2:
                            pe.wait_ge(s_e, i - 1)
                        for t in range(4):
                            last = nc.tensor.transpose(bank[i % 2][0:n, t * P:(t + 1) * P], kvT[:, t, i * P:i * P + n],
                                                       ident[:, :])
                        last.then_inc(s_t, 1)

                @block.vector
                def _(dve):
                    for i in range(ST + 1):
                        n = P if i < ST else NB
                        dve.wait_ge(s_t, i + 1)
                        nc.vector.tensor_copy(tokm[0:n, i, :], bank[i % 2][0:n, :]).then_inc(s_e, 1)

                @block.sync
                def _(sp):
                    for i in range(ST + 1):
                        sp.wait_ge(s_e, i + 1)
                        for half, outs in enumerate(((k_prompt, k_sample), (v_prompt, v_sample))):
                            if i < ST:
                                dst = outs[0][l, 0, i * P:(i + 1) * P].rearrange("t g d -> t (g d)")
                                src = tokm[:, i, half * KVD:(half + 1) * KVD]
                            else:
                                dst = outs[1][l, :, 0].rearrange("b g d -> b (g d)")
                                src = tokm[0:NB, ST, half * KVD:(half + 1) * KVD]
                            sp.dma_start(dst, src).then_inc(s_out, 16)
                    sp.wait_ge(s_out, 32 * (ST + 1))

        def project_out(l):
            view = w_o[l].rearrange("(k p) (t u n) -> p k t u n", p=P, u=2, n=GROUP_COLS)
            gemm(f"o{l}", D // (2 * GROUP_COLS),
                 lambda i, u: view[:, :, bass.ds(i, 1), u, :].rearrange("p k t n -> p k (t n)"), o_hi, o_lo,
                 lambda i, tile: nc.vector.tensor_tensor(cols3(xT[:, bass.ds(4 * i + tile, 1), :]), acc[tile % 2][:, :, 0:NG],
                                                         cols3(xT[:, bass.ds(4 * i + tile, 1), :]), ALU.add),
                 source=oT)

        def ffn_parameters(l):
            prow = at(f"prow{l}", [NPAR, F], C)
            s_in, s_t, s_e = sem(f"par_loaded_{l}"), sem(f"par_turned_{l}"), sem(f"par_copied_{l}")
            per_bank = 512 // NPAR
            with phase() as block:
                @block.sync
                def _(sp):
                    sp.dma_start(prow[0:2 * NB, :], state_conv[l].rearrange("b j f -> (b j) f")).then_inc(s_in, 16)
                    sp.dma_start(prow[2 * NB:2 * NB + 3, :], ffn_conv_w[l]).then_inc(s_in, 16)
                    sp.dma_start(prow[2 * NB + 3:NPAR, :], row(ffn_conv_b[l])).then_inc(s_in, 16)
                    sp.dma_start(conv_sample[l, :, 0, :], state_conv[l, :, 1, :]).then_inc(s_in, 16)
                    sp.wait_ge(s_in, 64)

                @block.tensor
                def _(pe):
                    pe.wait_ge(s_in, 64)
                    for f in range(FT):
                        last = nc.tensor.transpose(bank[f // per_bank][:, (f % per_bank) * NPAR:(f % per_bank + 1) * NPAR],
                                                   prow[:, f * P:(f + 1) * P], ident[0:NPAR, 0:NPAR])
                    last.then_inc(s_t, 1)

                @block.vector
                def _(dve):
                    dve.wait_ge(s_t, 1)
                    for b0 in range(0, FT, per_bank):
                        n = min(per_bank, FT - b0)
                        nc.vector.tensor_copy(fpar[:, b0:b0 + n, :].rearrange("p f r -> p (f r)"),
                                              bank[b0 // per_bank][:, 0:n * NPAR]).then_inc(s_e, 1)

        act_hi = at("act_hi", [P, 2, TOK], C, F32R)
        act_lo = at("act_lo", [P, 2, TOK], C + 2 * TILE, F32R)
        conv = [at(f"conv{m}", [P, TOK], C + (4 + m) * TILE) for m in range(2)]
        gate = [at(f"gate{m}", [P, TOK], C + (6 + m) * TILE) for m in range(2)]
        a_pad = [at(f"a_pad{m}", [P, TOK + 2], DD + m * (TILE + 32)) for m in range(2)]
        conv_rows = at("conv_rows", [P, 2, P], DD + 2 * (TILE + 32))

        def ffn(l):
            s_w, s_hi, s_lo = sem(f"ffn_w_loaded_{l}"), sem(f"ffn_w_hi_{l}"), sem(f"ffn_w_lo_{l}")
            s_a, s_b, s_down = sem(f"ffn_a_ready_{l}"), sem(f"ffn_b_ready_{l}"), sem(f"ffn_down_ready_{l}")
            s_acopy, s_gated, s_added = sem(f"ffn_a_copied_{l}"), sem(f"ffn_gated_{l}"), sem(f"ffn_added_{l}")
            s_tap, s_c1, s_conv, s_gelu = (sem(f"ffn_{n}_{l}") for n in ("tap2", "tap1", "conv", "gelu"))
            s_ahi, s_alo = sem(f"ffn_act_hi_{l}"), sem(f"ffn_act_lo_{l}")
            s_par, s_rt, s_rc = sem(f"ffn_par_{l}"), sem(f"ffn_rows_turned_{l}"), sem(f"ffn_rows_copied_{l}")
            s_out = [sem(f"ffn_rows_stored{m}_{l}") for m in range(2)]
            up = [w[l].rearrange("(k p) (i n) -> p k i n", p=P, n=GROUP_COLS) for w in (ffn_w_a, ffn_w_b)]
            down = ffn_w_down[l].rearrange("(i k p) n -> p i k n", k=2, p=P)
            state_p = conv_prompt[l, 0].rearrange("j (t n) -> j t n", n=P)
            state_s = conv_sample[l, :, 1, :].rearrange("b (t n) -> b t n", n=P)

            def as_down(t):
                return t[:, :, :].rearrange("p k n -> p (k n)").rearrange("p (k n) -> p k n", k=2)

            raw_down, down_hi, down_lo = as_down(raw), as_down(w_hi[2]), as_down(w_lo[2])
            END = CHUNKS - 1
            assert CHUNKS >= 2

            def over_chunks(engine, body):
                body(0, True, False)
                if CHUNKS > 2:
                    with engine.Fori(1, END) as i:
                        body(i, False, False)
                body(END, False, True)

            def number_down(i, last):
                return 3 * i + 2 if last else 3 * i + 3

            with phase() as block:
                @block.sync
                def _(sp):
                    def load(dst, src, n):
                        sp.wait_ge(s_lo, n + 1)
                        sp.dma_start(dst, src).then_inc(s_w, 16)

                    def load_up(u, i, n):
                        load(raw[:, :, :], up[u][:, :, bass.ds(i, 1), :].rearrange("p k t n -> p k (t n)"), n)

                    load_up(0, 0, 0)
                    load_up(1, 0, 1)

                    def body(i, first, last):
                        if not last:
                            load_up(0, i + 1, 3 * i + 2)
                        load(raw_down, down[:, bass.ds(i, 1), :, :].rearrange("p i k n -> p (i k) n"),
                             number_down(i, last))
                        if not last:
                            load_up(1, i + 1, 3 * i + 4)
                        for m in range(2):
                            sp.wait_ge(s_rc, 2 * i + m + 1)
                            sp.dma_start(state_p[:, bass.ds(2 * i + m, 1), :].rearrange("j t n -> j (t n)"),
                                         conv_rows[P - 2 - NB:P - NB, m, :]).then_inc(s_out[m], 16)
                            sp.dma_start(state_s[:, bass.ds(2 * i + m, 1), :].rearrange("j t n -> j (t n)"),
                                         conv_rows[P - NB:P, m, :]).then_inc(s_out[m], 16)

                    over_chunks(sp, body)
                    for m in range(2):
                        sp.wait_ge(s_out[m], 32 * CHUNKS)

                @block.scalar
                def _(act):
                    def hi_part(dst, src, n):
                        act.wait_ge(s_w, 16 * n + 16)
                        nc.scalar.activation(dst, src, ACT.Copy).then_inc(s_hi, 1)

                    for u in range(2):
                        hi_part(w_hi[u][:, :, :], raw[:, :, :], u)

                    def body(i, first, last):
                        for m in range(2):
                            act.wait_ge(s_a, 2 * i + m + 1)
                            if not first:
                                act.wait_ge(s_rt, 2 * i + m - 1)
                            nc.scalar.activation(a_pad[m][:, 2:2 + TOK].rearrange("p (c n) -> p c n", c=CG),
                                                 acc[0][:, :, 0:NG], ACT.Copy).then_inc(s_acopy, 1)
                            if m == 1 and not last:
                                hi_part(w_hi[0][:, :, :], raw[:, :, :], 3 * i + 2)
                            act.wait_ge(s_par, i + 1)
                            act.wait_ge(s_acopy, 2 * i + m + 1)
                            nc.scalar.activation(conv[m][:, :], a_pad[m][:, 2:2 + TOK], ACT.Identity,
                                                 scale=fcur[:, m, 2 * NB + 2:2 * NB + 3],
                                                 bias=fcur[:, m, 2 * NB + 3:NPAR]).then_inc(s_tap, 1)
                            act.wait_ge(s_conv, 2 * i + m + 1)
                            nc.scalar.activation(conv[m][:, :], conv[m][:, :], ACT.Gelu_apprx_tanh).then_inc(s_gelu, 1)
                            act.wait_ge(s_gated, 2 * i + m + 1)
                            nc.scalar.activation(act_hi[:, m, :], gate[m][:, :], ACT.Copy).then_inc(s_ahi, 1)
                        hi_part(down_hi, raw_down, number_down(i, last))
                        if not last:
                            hi_part(w_hi[1][:, :, :], raw[:, :, :], 3 * i + 4)

                    over_chunks(act, body)

                @block.gpsimd
                def _(pool):
                    pool.sem_inc(s_lo, 1)

                    def lo_part(dst, src, hi, n):
                        pool.wait_ge(s_hi, n + 1)
                        nc.gpsimd.tensor_tensor(dst, src, hi, ALU.subtract).then_inc(s_lo, 1)

                    for u in range(2):
                        lo_part(w_lo[u][:, :, :], raw[:, :, :], w_hi[u][:, :, :].bitcast(F32), u)

                    def body(i, first, last):
                        for m in range(2):
                            if m == 1 and not last:
                                lo_part(w_lo[0][:, :, :], raw[:, :, :], w_hi[0][:, :, :].bitcast(F32), 3 * i + 2)
                            pool.wait_ge(s_ahi, 2 * i + m + 1)
                            nc.gpsimd.tensor_tensor(act_lo[:, m, :], gate[m][:, :], act_hi[:, m, :].bitcast(F32),
                                                    ALU.subtract).then_inc(s_alo, 1)
                        lo_part(down_lo, raw_down, down_hi.bitcast(F32), number_down(i, last))
                        if not last:
                            lo_part(w_lo[1][:, :, :], raw[:, :, :], w_hi[1][:, :, :].bitcast(F32), 3 * i + 4)

                    over_chunks(pool, body)

                @block.vector
                def _(dve):
                    for m in range(2):
                        nc.vector.memset(a_pad[m][:, 0:2], 0.0)

                    def add_down(i):
                        for t in range(KT):
                            dve.wait_ge(s_down, KT * i + t + 1)
                            side = t % 2 if isinstance(i, int) and i == END else (t + 1) % 2
                            nc.vector.tensor_tensor(cols3(xT[:, t:t + 1, :]), acc[side][:, :, 0:NG], cols3(xT[:, t:t + 1, :]),
                                                    ALU.add).then_inc(s_added, 1)

                    def body(i, first, last):
                        nc.vector.tensor_copy(fcur[:, :, :], fpar[:, bass.ds(2 * i, 2), :]).then_inc(s_par, 1)
                        for m in range(2):
                            def tap(j):
                                return fcur[:, m, 2 * NB + j:2 * NB + j + 1]
                            state = fcur[:, m, 0:2 * NB].rearrange("p (b j) -> p j b", j=2)
                            dve.wait_ge(s_par, i + 1)
                            dve.wait_ge(s_tap, 2 * i + m + 1)
                            nc.vector.scalar_tensor_tensor(out=conv[m][:, 0:SEQ], in0=a_pad[m][:, 1:1 + SEQ], scalar=tap(1),
                                                           in1=conv[m][:, 0:SEQ], op0=ALU.mult, op1=ALU.add)
                            nc.vector.scalar_tensor_tensor(out=conv[m][:, SEQ:TOK], in0=state[:, 1, :], scalar=tap(1),
                                                           in1=conv[m][:, SEQ:TOK], op0=ALU.mult, op1=ALU.add).then_inc(s_c1, 1)
                            dve.wait_ge(s_c1, 2 * i + m + 1)
                            nc.vector.scalar_tensor_tensor(out=conv[m][:, SEQ:TOK], in0=state[:, 0, :], scalar=tap(0),
                                                           in1=conv[m][:, SEQ:TOK], op0=ALU.mult, op1=ALU.add)
                            nc.vector.scalar_tensor_tensor(out=conv[m][:, 0:SEQ], in0=a_pad[m][:, 0:SEQ], scalar=tap(0),
                                                           in1=conv[m][:, 0:SEQ], op0=ALU.mult, op1=ALU.add).then_inc(s_conv, 1)
                            if m == 0 and not first:
                                add_down(i - 1)
                            dve.wait_ge(s_b, 2 * i + m + 1)
                            dve.wait_ge(s_gelu, 2 * i + m + 1)
                            if not first:
                                dve.wait_ge(s_alo, 2 * i + m - 1)
                            nc.vector.tensor_tensor(gate[m][:, :].rearrange("p (c n) -> p c n", c=CG), acc[1][:, :, 0:NG],
                                                    conv[m][:, :].rearrange("p (c n) -> p c n", c=CG),
                                                    ALU.mult).then_inc(s_gated, 1)
                            dve.wait_ge(s_rt, 2 * i + m + 1)
                            if not first:
                                dve.wait_ge(s_out[m], 32 * i)
                            nc.vector.tensor_copy(conv_rows[:, m, :], bank[m][:, 0:P]).then_inc(s_rc, 1)

                    over_chunks(dve, body)
                    add_down(END)

                @block.tensor
                def _(pe):
                    def down_products(i, last):
                        pe.wait_ge(s_lo, number_down(i, last) + 2)
                        pe.wait_ge(s_alo, 2 * i + 2)
                        for t in range(KT):
                            if t >= 2:
                                pe.wait_ge(s_added, KT * i + t - 1)
                            elif (t == 0) == last:
                                pe.wait_ge(s_acopy, 2 * i + 2 if last else 2 * i + 3)
                            else:
                                pe.wait_ge(s_gated, 2 * i + 2)
                            side = t % 2 if last else (t + 1) % 2
                            split_product(acc[side], down_hi, down_lo, slice(t * P, (t + 1) * P),
                                          act_hi, act_lo, 2).then_inc(s_down, 1)

                    def rows(i, m, first):
                        pe.wait_ge(s_acopy, 2 * i + m + 1)
                        if not first:
                            pe.wait_ge(s_rc, 2 * i + m - 1)
                        nc.tensor.transpose(bank[m][:, 0:P], a_pad[m][:, 2 + TOK - P:2 + TOK], ident[:, :]).then_inc(s_rt, 1)

                    def body(i, first, last):
                        pe.wait_ge(s_lo, 2 if first else 3 * i + 1)
                        if not first:
                            pe.wait_ge(s_acopy, 2 * i)
                        split_product(acc[0], w_hi[0], w_lo[0], slice(0, P), h_hi, h_lo, KT).then_inc(s_a, 1)
                        if not first:
                            down_products(i - 1, False)
                            pe.wait_ge(s_added, KT * i - 1)
                        rows(i, 0, first)
                        pe.wait_ge(s_lo, 3 if first else 3 * i + 3)
                        split_product(acc[1], w_hi[1], w_lo[1], slice(0, P), h_hi, h_lo, KT).then_inc(s_b, 1)
                        if not first:
                            pe.wait_ge(s_added, KT * i)
                        pe.wait_ge(s_acopy, 2 * i + 1)
                        split_product(acc[0], w_hi[0], w_lo[0], slice(P, 2 * P), h_hi, h_lo, KT).then_inc(s_a, 1)
                        pe.wait_ge(s_gated, 2 * i + 1)
                        split_product(acc[1], w_hi[1], w_lo[1], slice(P, 2 * P), h_hi, h_lo, KT).then_inc(s_b, 1)
                        rows(i, 1, first)

                    over_chunks(pe, body)
                    down_products(END, True)

        def store_y():
            yrow = at("yrow", [P, 2, D], A)
            s_t, s_e = sem("y_turned"), sem("y_copied")
            s_out = [sem(f"y_stored{u}") for u in range(2)]
            with phase() as block:
                @block.tensor
                def _(pe):
                    for i in range(ST + 1):
                        n = P if i < ST else NB
                        if i >= 2:
                            pe.wait_ge(s_e, i - 1)
                        for c in range(KT):
                            last = nc.tensor.transpose(acc[i % 2][0:n, c // 4, (c % 4) * P:(c % 4 + 1) * P],
                                                       xT[:, c, i * P:i * P + n], ident[:, :])
                        last.then_inc(s_t, 1)

                @block.vector
                def _(dve):
                    for i in range(ST + 1):
                        n = P if i < ST else NB
                        dve.wait_ge(s_t, i + 1)
                        if i >= 2:
                            dve.wait_ge(s_out[i % 2], 16 * (i // 2))
                        nc.vector.tensor_copy(yrow[0:n, i % 2, :].rearrange("p (c n) -> p c n", c=2),
                                              acc[i % 2][0:n, 0:2, :]).then_inc(s_e, 1)

                @block.sync
                def _(sp):
                    for i in range(ST + 1):
                        sp.wait_ge(s_e, i + 1)
                        if i < ST:
                            sp.dma_start(y_prompt[0, i * P:(i + 1) * P, :], yrow[:, i % 2, :]).then_inc(s_out[i % 2], 16)
                        else:
                            sp.dma_start(y_sample[:, 0, :], yrow[0:NB, i % 2, :]).then_inc(s_out[i % 2], 16)
                    for u in range(2):
                        sp.wait_ge(s_out[u], 16 * ((ST + 2 - u) // 2))

        def log_forget():
            wf = at("wf", [P, KT, NH], W)
            wf_hi = at("wf_hi", [P, KT, P], W + KT * P * 4, F32R)
            wf_lo = at("wf_lo", [P, KT, P], W + 2 * KT * P * 4, F32R)
            t0 = W + 3 * KT * P * 4
            zb, e, cum, one = (at(f"lf_{n}", [NH, TOK], t0 + j * TILE) for j, n in enumerate(("z", "e", "cum", "one")))
            lrow = at("lf_row", [P, ST + 1, NH], t0 + 4 * TILE)
            bias = at("lf_bias", [NH, 1], t0 + 4 * TILE + (ST + 1) * NH * 4)
            s_in, s_clear, s_hi, s_lo = sem("lf_loaded"), sem("lf_clear"), sem("lf_w_hi"), sem("lf_w_lo")
            s_mm, s_act, s_dve, s_t, s_out = sem("lf_product"), sem("lf_act"), sem("lf_dve"), sem("lf_turned"), sem("lf_stored")
            with phase() as block:
                @block.sync
                def _(sp):
                    sp.dma_start(wf[:, :, :], fox_w_f.rearrange("(k p) h -> p k h", p=P)).then_inc(s_in, 16)
                    sp.dma_start(bias[:, :], fox_b_f.rearrange("(h a) -> h a", a=1)).then_inc(s_in, 16)
                    sp.wait_ge(s_dve, 4)
                    sp.dma_start(logf_prompt[0].rearrange("(i p) h -> p i h", p=P), lrow[:, 0:ST, :]).then_inc(s_out, 16)
                    sp.dma_start(logf_sample[:, 0, :], lrow[0:NB, ST, :]).then_inc(s_out, 16)
                    sp.dma_start(ncum_dram, cum[:, 0:SEQ]).then_inc(s_out, 16)
                    sp.wait_ge(s_out, 48)

                @block.gpsimd
                def _(pool):
                    nc.gpsimd.memset(wf_hi[:, :, :].bitcast(F32), 0.0).then_inc(s_clear, 1)
                    nc.gpsimd.memset(wf_lo[:, :, :].bitcast(F32), 0.0).then_inc(s_clear, 1)
                    nc.gpsimd.memset(one[:, :], 1.0).then_inc(s_clear, 1)

                @block.scalar
                def _(act):
                    nc.scalar.preload_act_table_set(EXP_LN_SET)
                    act.wait_ge(s_in, 32)
                    act.wait_ge(s_clear, 3)
                    nc.scalar.activation(wf_hi[:, :, 0:NH], wf[:, :, :], ACT.Copy).then_inc(s_hi, 1)
                    act.wait_ge(s_mm, 1)
                    nc.scalar.activation(zb[:, :].rearrange("p (c n) -> p c n", c=CG), acc[0][0:NH, :, 0:NG],
                                         ACT.Identity, bias=bias[:, :]).then_inc(s_act, 1)
                    act.wait_ge(s_act, 1)
                    nc.scalar.activation(e[:, :], zb[:, :], ACT.Abs).then_inc(s_act, 1)
                    act.wait_ge(s_act, 2)
                    nc.scalar.activation(e[:, :], e[:, :], ACT.Exp, scale=-1.0).then_inc(s_act, 1)
                    act.wait_ge(s_act, 3)
                    nc.scalar.activation(e[:, :], e[:, :], ACT.Ln, bias=1.0).then_inc(s_act, 1)

                @block.tensor
                def _(pe):
                    pe.wait_ge(s_lo, 1)
                    split_product(acc[0], wf_hi, wf_lo, slice(0, P), h_hi, h_lo, KT).then_inc(s_mm, 1)
                    pe.wait_ge(s_dve, 1)
                    for i in range(ST + 1):
                        n = P if i < ST else NB
                        last = nc.tensor.transpose(bank[0][0:n, i * NH:(i + 1) * NH], zb[:, i * P:i * P + n],
                                                   ident[0:NH, 0:NH])
                    last.then_inc(s_t, 1)

                @block.vector
                def _(dve):
                    dve.wait_ge(s_hi, 1)
                    nc.vector.tensor_tensor(wf_lo[:, :, 0:NH], wf[:, :, :], wf_hi[:, :, 0:NH].bitcast(F32),
                                            ALU.subtract).then_inc(s_lo, 1)
                    dve.wait_ge(s_act, 4)
                    nc.vector.scalar_tensor_tensor(out=zb[:, :], in0=zb[:, :], scalar=0.0, in1=e[:, :],
                                                   op0=ALU.min, op1=ALU.subtract).then_inc(s_dve, 1)
                    dve.wait_ge(s_dve, 1)
                    nc.vector.tensor_tensor_scan(cum[:, 0:SEQ], one[:, 0:SEQ], zb[:, 0:SEQ], 0.0,
                                                 ALU.mult, ALU.add).then_inc(s_dve, 1)
                    dve.wait_ge(s_dve, 2)
                    nc.vector.tensor_scalar(cum[:, 0:SEQ], cum[:, 0:SEQ], -1.0, None, ALU.mult).then_inc(s_dve, 1)
                    dve.wait_ge(s_t, 1)
                    nc.vector.tensor_copy(lrow[:, 0:ST, :].rearrange("p i h -> p (i h)"), bank[0][:, 0:ST * NH])
                    nc.vector.tensor_copy(lrow[0:NB, ST, :], bank[0][0:NB, ST * NH:(ST + 1) * NH]).then_inc(s_dve, 1)

        TOKM = (ST + 1) * 2 * KVD * 4
        kcur = at("kcur", [P, 2, SEQ], W + TOKM)
        vcur = at("vcur", [P, ST, P], W + TOKM + 2 * SEQ * 4)
        qcur = [at(f"qcur{s}", [P, SEQ], W + TOKM + (3 + s) * SEQ * 4) for s in range(2)]
        WT = W + TOKM + 5 * SEQ * 4
        PAIRS = 2 * HG // 2
        STEPS = 2 * HG * ST
        TURNS = NKV // 2
        v_tiles = tokm[:, 0:ST, :].rearrange("p i (c n) -> p i c n", n=P)
        MULT1 = dict(scalar1=1.0, scalar2=None, op0=ALU.mult)

        def copy_keys_values(t):
            for gp in range(2):
                for side in range(2):
                    nc.vector.tensor_scalar(kcur[side * HALF:(side + 1) * HALF, gp, :],
                                            kvT[gp * HALF:(gp + 1) * HALF, bass.ds(t, 1), 0:SEQ].rearrange("p a n -> p (a n)"),
                                            **MULT1)
            return nc.vector.tensor_scalar(vcur[:, :, :], v_tiles[:, :, bass.ds(t + 2, 1), :].rearrange("p i a n -> p i (a n)"),
                                           **MULT1)

        def copy_queries(t, pr):
            return nc.vector.tensor_scalar(qcur[pr % 2][:, :],
                                           qT[:, bass.ds(PAIRS * t + pr, 1), 0:SEQ].rearrange("p a n -> p (a n)"), **MULT1)

        def half(hh):
            return slice((hh % 2) * HALF, (hh % 2 + 1) * HALF)

        def pieces(a, b):
            while a < b:
                e = min(b, (a // 512 + 1) * 512)
                yield a, e
                a = e

        def stick_prompt():
            tiles = [B + j * SEQ * 4 for j in range(8)] + [WT + j * SEQ * 4 for j in range(4)]
            zs, ea, sp_ = ([at(f"{n}{j}", [P, SEQ], tiles[4 * m + j]) for j in range(4)]
                           for m, n in enumerate(("st_z", "st_e", "st_sp")))
            z_ps = [flat(0, 2), flat(2, 4)]
            r_ps, o_ps = flat(4, 6), flat(6, 8)
            s_turn, s_cur, s_seen = sem("st_turn"), sem("st_copied"), sem("st_waits_seen")
            s_z, s_zc, s_e1, s_ln = sem("st_z_ready"), sem("st_z_copied"), sem("st_act"), sem("st_ln")
            s_sp, s_spm, s_r, s_arg = sem("st_sp"), sem("st_sp_masked"), sem("st_r_ready"), sem("st_arg")
            s_w, s_argm, s_pv, s_o = sem("st_w"), sem("st_arg_masked"), sem("st_pv"), sem("st_o_copied")

            def key_block(n):
                return ST - 1 - n % ST

            def head(n):
                return n // ST

            def first_in_bank(b, col):
                return b == min(ST - 1, 4 * (col // 512) + 3)

            with phase() as block:
                @block.tensor
                def _(pe):
                    pe.sem_inc(s_turn, 1)

                    def scores(t, n):
                        b, hh = key_block(n), head(n)
                        if n % (2 * ST) == 0:
                            pe.wait_ge(s_cur, 5 * t + 2 + hh // 2)
                        if n >= 2:
                            pe.wait_ge(s_zc, t * STEPS + n - 1)
                        for c0, c1 in pieces(b * P, SEQ):
                            last = nc.tensor.matmul(z_ps[n % 2][:, c0:c1], kcur[half(hh), hh // HG, b * P:(b + 1) * P],
                                                    qcur[hh // 2 % 2][half(hh), c0:c1], start=True, stop=True)
                        last.then_inc(s_z, 1)

                    def add_to_r(n, tri, first):
                        b = key_block(n)
                        for c0, c1 in pieces(b * P, SEQ):
                            last = nc.tensor.matmul(r_ps[:, c0:c1], tri[:, :], sp_[n % 4][:, c0:c1],
                                                    start=first and first_in_bank(b, c0), stop=True, skip_group_check=True)
                        return last

                    def values(t, n):
                        b, hh = key_block(n), head(n)
                        pe.wait_ge(s_w, t * STEPS + n + 1)
                        if n % ST == 0 and hh >= 1:
                            pe.wait_ge(s_o, 2 * HG * t + hh)
                        gp = hh // HG
                        for c0, c1 in pieces(b * P, SEQ):
                            last = nc.tensor.matmul(o_ps[0:HALF, c0:c1], vcur[:, b, gp * HALF:(gp + 1) * HALF],
                                                    ea[n % 4][:, c0:c1], start=first_in_bank(b, c0), stop=True,
                                                    skip_group_check=True)
                        last.then_inc(s_pv, 1)

                    with pe.Fori(0, TURNS) as t:
                        scores(t, 0)
                        scores(t, 1)
                        for n in range(STEPS):
                            if n + 2 < STEPS:
                                scores(t, n + 2)
                            pe.wait_ge(s_spm, t * STEPS + n + 1)
                            add_to_r(n, tri_incl, True).then_inc(s_r, 1)
                            if n >= 2:
                                values(t, n - 2)
                            pe.wait_ge(s_arg, t * STEPS + n + 1)
                            if key_block(n) > 0:
                                add_to_r(n, tri_comp, False)
                        values(t, STEPS - 2)
                        values(t, STEPS - 1)
                        pe.wait_ge(s_pv, (t + 1) * STEPS)
                        pe.sem_inc(s_turn, 1)

                @block.vector
                def _(dve):
                    def copy_scores(t, n):
                        b = key_block(n)
                        dve.wait_ge(s_z, t * STEPS + n + 1)
                        nc.vector.tensor_copy(zs[n % 4][:, b * P:SEQ], z_ps[n % 2][:, b * P:SEQ]).then_inc(s_zc, 1)
                        if n % (2 * ST) == 2 * ST - 1 and n // (2 * ST) + 2 < PAIRS:
                            copy_queries(t, n // (2 * ST) + 2).then_inc(s_cur, 1)

                    def softplus(t, n):
                        b = key_block(n)
                        dve.wait_ge(s_ln, t * STEPS + n + 1)
                        nc.vector.scalar_tensor_tensor(out=sp_[n % 4][:, b * P:SEQ], in0=zs[n % 4][:, b * P:SEQ], scalar=0.0,
                                                       in1=ea[n % 4][:, b * P:SEQ], op0=ALU.max, op1=ALU.add).then_inc(s_sp, 1)

                    def argument(t, n):
                        b = key_block(n)
                        dve.wait_ge(s_r, t * STEPS + n + 1)
                        nc.vector.tensor_tensor(ea[n % 4][:, b * P:SEQ], zs[n % 4][:, b * P:SEQ], r_ps[:, b * P:SEQ],
                                                ALU.subtract).then_inc(s_arg, 1)

                    def store_o(t, hh):
                        dve.wait_ge(s_pv, t * STEPS + (hh + 1) * ST)
                        nc.vector.tensor_scalar(oT[half(hh), bass.ds(PAIRS * t + hh // 2, 1), 0:SEQ].rearrange("p a n -> p (a n)"),
                                                o_ps[0:HALF, 0:SEQ], **MULT1).then_inc(s_o, 1)

                    with dve.Fori(0, TURNS) as t:
                        dve.wait_ge(s_turn, t + 1)
                        copy_keys_values(t).then_inc(s_cur, 1)
                        copy_queries(t, 0).then_inc(s_cur, 1)
                        copy_queries(t, 1).then_inc(s_cur, 1)
                        copy_scores(t, 0)
                        copy_scores(t, 1)
                        softplus(t, 0)
                        for n in range(STEPS):
                            if n + 2 < STEPS:
                                copy_scores(t, n + 2)
                            if n + 1 < STEPS:
                                softplus(t, n + 1)
                            argument(t, n)
                            if n >= 2 and (n - 2) % ST == ST - 1:
                                store_o(t, head(n - 2))
                        store_o(t, 2 * HG - 1)

                @block.scalar
                def _(act):
                    nc.scalar.preload_act_table_set(EXP_LN_SET)

                    def log_part(t, n):
                        b = key_block(n)
                        e = ea[n % 4][:, b * P:SEQ]
                        act.wait_ge(s_zc, t * STEPS + n + 1)
                        if n >= 4:
                            act.wait_ge(s_pv, t * STEPS + n - 3)
                        nc.scalar.activation(e, zs[n % 4][:, b * P:SEQ], ACT.Abs).then_inc(s_e1, 1)
                        act.wait_ge(s_e1, 2 * (t * STEPS + n) + 1)
                        nc.scalar.activation(e, e, ACT.Exp, scale=-1.0).then_inc(s_e1, 1)
                        act.wait_ge(s_e1, 2 * (t * STEPS + n) + 2)
                        nc.scalar.activation(e, e, ACT.Ln, bias=1.0).then_inc(s_ln, 1)

                    def weights(t, n):
                        b = key_block(n)
                        act.wait_ge(s_argm, t * STEPS + n + 1)
                        nc.scalar.activation(ea[n % 4][:, b * P:SEQ], ea[n % 4][:, b * P:SEQ], ACT.Exp).then_inc(s_w, 1)

                    with act.Fori(0, TURNS) as t:
                        log_part(t, 0)
                        for n in range(STEPS):
                            if n + 1 < STEPS:
                                log_part(t, n + 1)
                            if n >= 1:
                                weights(t, n - 1)
                        weights(t, STEPS - 1)

                @block.gpsimd
                def _(pool):
                    def mask(tile, n, value, done):
                        d = tile[n % 4][:, key_block(n) * P:(key_block(n) + 1) * P]
                        nc.gpsimd.affine_select(out=d, in_=d, compare_op=ALU.is_ge, fill=value, base=-1,
                                                pattern=[[1, P]], channel_multiplier=-1).then_inc(done, 1)

                    def mask_sp(t, n):
                        pool.wait_ge(s_sp, t * STEPS + n + 1)
                        pool.sem_inc(s_seen, 1)
                        mask(sp_, n, 0.0, s_spm)

                    def mask_argument(t, n):
                        pool.wait_ge(s_arg, t * STEPS + n + 1)
                        pool.sem_inc(s_seen, 1)
                        mask(ea, n, NEG, s_argm)

                    with pool.Fori(0, TURNS) as t:
                        mask_sp(t, 0)
                        for n in range(STEPS):
                            if n + 1 < STEPS:
                                mask_sp(t, n + 1)
                            mask_argument(t, n)

        def fox_prompt():
            tiles = [B + j * SEQ * 4 for j in range(8)]
            pt, tp = [at(f"fx_p{j}", [P, SEQ], tiles[j]) for j in range(2)], [at(f"fx_pT{j}", [P, SEQ], tiles[2 + j]) for j in range(2)]
            ncum = [at(f"fx_ncum{j}", [P, SEQ], tiles[4 + j]) for j in range(2)]
            opair = [at(f"fx_o{j}", [P, ST, P], tiles[6 + j]) for j in range(2)]
            stat = at("fx_stat", [P, 4, 4], WT)
            s_ps = [flat(0, 2), flat(2, 4)]
            t_ps = [psum[:, 4, :], psum[:, 5, :]]
            o_ps = [psum[:, 6, :], psum[:, 7, :]]
            s_turn, s_cur, s_seen = sem("fx_turn"), sem("fx_copied"), sem("fx_waits_seen")
            s_nc = [sem(f"fx_ncum_loaded{j}") for j in range(2)]
            s_s, s_max, s_nmax, s_p = sem("fx_scores"), sem("fx_max"), sem("fx_neg_max"), sem("fx_probs")
            s_t, s_ta, s_tv = sem("fx_turned"), sem("fx_turned_copied_act"), sem("fx_turned_copied_dve")
            s_pv, s_rc, s_o = sem("fx_pv"), sem("fx_recip"), sem("fx_o_copied")

            groups, of_step, of_pair = [], {}, {}

            def add_group(key, table, j, engine):
                table.setdefault(key, []).append(len(groups))
                groups.append((key, j, engine))

            def plan():
                for n in range(STEPS + 2):
                    if n < STEPS:
                        for j in range(0, n % ST + 1, 4):
                            add_group(n, of_step, j, "act" if len(groups) % 2 else "dve")
                    if n >= 2 and (n - 2) % (2 * ST) == 2 * ST - 1:
                        for j in range(0, ST, 4):
                            add_group((n - 2) // (2 * ST), of_pair, j, "dve")

            plan()
            GROUPS = len(groups)

            def copies(engine, upto):
                return sum(1 for g in groups[:upto + 1] if g[2] == engine)

            ALL = {e: copies(e, GROUPS - 1) for e in ("act", "dve")}

            with phase() as block:
                @block.sync
                def _(sp):
                    with sp.Fori(0, TURNS) as t:
                        for hh in range(2 * HG):
                            if hh < 2:
                                sp.wait_ge(s_turn, t + 1)
                            else:
                                sp.wait_ge(s_max, t * STEPS + (hh - 1) * ST)
                            sp.dma_start(ncum[hh % 2][:, :], ncum_dram[bass.ds(2 * HG * t + hh, 1), :].partition_broadcast(P))\
                                .then_inc(s_nc[hh % 2], 16)

                @block.tensor
                def _(pe):
                    pe.sem_inc(s_turn, 1)

                    def scores(t, n):
                        i, hh = n % ST, n // ST
                        if n % (2 * ST) == 0:
                            pe.wait_ge(s_cur, 5 * t + 2 + hh // 2)
                        if n >= 2:
                            pe.wait_ge(s_max, t * STEPS + n - 1)
                        q = qcur[hh // 2 % 2][half(hh), i * P:(i + 1) * P]
                        for c0, c1 in pieces(0, (i + 1) * P):
                            nc.tensor.matmul(s_ps[n % 2][:, c0:c1], q, kcur[half(hh), hh // HG, c0:c1],
                                             start=True, stop=True)
                        nc.tensor.matmul(s_ps[n % 2][:, i * P:(i + 1) * P], ident[:, :], causal[:, :], start=False, stop=True,
                                         skip_group_check=True).then_inc(s_s, 1)

                    def bank_free(t, g):
                        if g >= 2:
                            e = groups[g - 2][2]
                            pe.wait_ge(s_ta if e == "act" else s_tv, t * ALL[e] + copies(e, g - 2))

                    def turn_probs(t, n):
                        i = n % ST
                        pe.wait_ge(s_p, t * STEPS + n + 1)
                        for g in of_step[n]:
                            bank_free(t, g)
                            j0 = groups[g][1]
                            for j in range(j0, min(j0 + 4, i + 1)):
                                last = nc.tensor.transpose(t_ps[g % 2][:, (j - j0) * P:(j - j0 + 1) * P],
                                                           pt[n % 2][:, j * P:(j + 1) * P], ident[:, :])
                            last.then_inc(s_t, 1)

                    def turn_outputs(t, pr):
                        pe.wait_ge(s_o, t * STEPS + (pr + 1) * 2 * ST)
                        for g in of_pair[pr]:
                            bank_free(t, g)
                            j0 = groups[g][1]
                            for j in range(j0, min(j0 + 4, ST)):
                                last = nc.tensor.transpose(t_ps[g % 2][:, (j - j0) * P:(j - j0 + 1) * P],
                                                           opair[pr % 2][:, j, :], ident[:, :])
                            last.then_inc(s_t, 1)

                    def values(t, n):
                        i, hh = n % ST, n // ST
                        gs = of_step[n]
                        for e, s in (("act", s_ta), ("dve", s_tv)):
                            if any(groups[g][2] == e for g in gs):
                                pe.wait_ge(s, t * ALL[e] + copies(e, gs[-1]))
                        if n >= 2:
                            pe.wait_ge(s_o, t * STEPS + n - 1)
                        gp = hh // HG
                        for j in range(i + 1):
                            last = nc.tensor.matmul(o_ps[n % 2][:, 0:HALF], tp[n % 2][:, j * P:(j + 1) * P],
                                                    vcur[:, j, gp * HALF:(gp + 1) * HALF], start=(j == 0), stop=(j == i))
                        last.then_inc(s_pv, 1)

                    with pe.Fori(0, TURNS) as t:
                        scores(t, 0)
                        for n in range(STEPS + 2):
                            if n + 1 < STEPS:
                                scores(t, n + 1)
                            if 1 <= n <= STEPS:
                                values(t, n - 1)
                            if n < STEPS:
                                turn_probs(t, n)
                            if n >= 2 and (n - 2) % (2 * ST) == 2 * ST - 1:
                                turn_outputs(t, (n - 2) // (2 * ST))
                        pe.wait_ge(s_tv, (t + 1) * ALL["dve"])
                        pe.sem_inc(s_turn, 1)

                @block.vector
                def _(dve):
                    def add_decay(t, n):
                        i, hh = n % ST, n // ST
                        L = (i + 1) * P
                        if i == 0:
                            dve.wait_ge(s_nc[hh % 2], 16 * (HG * t + hh // 2 + 1))
                        if n >= 2:
                            dve.wait_ge(s_t, t * GROUPS + of_step[n - 2][-1] + 1)
                        dve.wait_ge(s_s, t * STEPS + n + 1)
                        dve.sem_inc(s_seen, 1)
                        st = stat[:, n % 4, :]
                        nc.vector.tensor_tensor_reduce(pt[n % 2][:, 0:L], s_ps[n % 2][:, 0:L], ncum[hh % 2][:, 0:L], 1.0, -3.0e38,
                                                       ALU.add, ALU.max, st[:, 0:1]).then_inc(s_max, 1)
                        dve.wait_ge(s_max, t * STEPS + n + 1)
                        nc.vector.tensor_scalar(st[:, 1:2], st[:, 0:1], -1.0, None, ALU.mult).then_inc(s_nmax, 1)

                    def copy_step(t, n):
                        for g in of_step[n]:
                            if groups[g][2] == "dve":
                                dve.wait_ge(s_t, t * GROUPS + g + 1)
                                j0 = groups[g][1]
                                w = (min(j0 + 4, n % ST + 1) - j0) * P
                                if n >= 2:
                                    dve.wait_ge(s_pv, t * STEPS + n - 1)
                                nc.vector.tensor_copy(tp[n % 2][:, j0 * P:j0 * P + w], t_ps[g % 2][:, 0:w]).then_inc(s_tv, 1)

                    def copy_pair(t, pr):
                        for g in of_pair[pr]:
                            dve.wait_ge(s_t, t * GROUPS + g + 1)
                            j0 = groups[g][1]
                            w = (min(j0 + 4, ST) - j0) * P
                            nc.vector.tensor_scalar(oT[:, bass.ds(PAIRS * t + pr, 1), j0 * P:j0 * P + w].rearrange("p a n -> p (a n)"),
                                                    t_ps[g % 2][:, 0:w], **MULT1).then_inc(s_tv, 1)

                    def normalise(t, n):
                        i, hh = n % ST, n // ST
                        st = stat[:, n % 4, :]
                        dve.wait_ge(s_p, t * STEPS + n + 1)
                        nc.vector.reciprocal(st[:, 3:4], st[:, 2:3]).then_inc(s_rc, 1)
                        if hh >= 4 and n % (2 * ST) == 0:
                            dve.wait_ge(s_t, t * GROUPS + of_pair[hh // 2 - 2][-1] + 1)
                        dve.wait_ge(s_rc, t * STEPS + n + 1)
                        dve.wait_ge(s_pv, t * STEPS + n + 1)
                        nc.vector.tensor_scalar(opair[hh // 2 % 2][:, i, half(hh)], o_ps[n % 2][:, 0:HALF], st[:, 3:4], None,
                                                ALU.mult).then_inc(s_o, 1)

                    with dve.Fori(0, TURNS) as t:
                        dve.wait_ge(s_turn, t + 1)
                        copy_keys_values(t).then_inc(s_cur, 1)
                        copy_queries(t, 0).then_inc(s_cur, 1)
                        copy_queries(t, 1).then_inc(s_cur, 1)
                        add_decay(t, 0)
                        for n in range(STEPS + 2):
                            if n + 1 < STEPS:
                                add_decay(t, n + 1)
                                if (n + 1) % (2 * ST) == 2 * ST - 1 and (n + 1) // (2 * ST) + 2 < PAIRS:
                                    copy_queries(t, (n + 1) // (2 * ST) + 2).then_inc(s_cur, 1)
                            if 1 <= n <= STEPS:
                                normalise(t, n - 1)
                            if n < STEPS:
                                copy_step(t, n)
                            if n >= 2 and (n - 2) % (2 * ST) == 2 * ST - 1:
                                copy_pair(t, (n - 2) // (2 * ST))

                @block.scalar
                def _(act):
                    def probs(t, n):
                        L = (n % ST + 1) * P
                        st = stat[:, n % 4, :]
                        act.wait_ge(s_nmax, t * STEPS + n + 1)
                        nc.scalar.activation(pt[n % 2][:, 0:L], pt[n % 2][:, 0:L], ACT.Exp, bias=st[:, 1:2],
                                             accum_out=st[:, 2:3]).then_inc(s_p, 1)

                    def copy_step(t, n):
                        for g in of_step[n]:
                            if groups[g][2] == "act":
                                j0 = groups[g][1]
                                w = (min(j0 + 4, n % ST + 1) - j0) * P
                                act.wait_ge(s_t, t * GROUPS + g + 1)
                                if n >= 2:
                                    act.wait_ge(s_pv, t * STEPS + n - 1)
                                nc.scalar.activation(tp[n % 2][:, j0 * P:j0 * P + w], t_ps[g % 2][:, 0:w], ACT.Copy)\
                                    .then_inc(s_ta, 1)

                    with act.Fori(0, TURNS) as t:
                        probs(t, 0)
                        for n in range(STEPS):
                            if n + 1 < STEPS:
                                probs(t, n + 1)
                            copy_step(t, n)

        HALVES = 2
        HH = NH // HALVES
        QUADS = NPAGE // 4
        COLS = NB * NPAGE * NH
        assert NPAGE % 4 == 0 and QUADS % 2 == 0 and NB % 2 == 0 and COLS <= 2048 and NB * NH == P

        def decode(l):
            fox = l == 1
            PG = NPAGE + 1 if fox else NPAGE
            off = [W]

            def tile(name, shape, dt=F32):
                n = 4
                for x in shape[1:]:
                    n *= x
                t = at(f"dc_{name}{l}", shape, off[0], dt)
                off[0] += n + (-n % 32)
                assert off[0] <= W + WBYTES
                return t

            page = [tile(f"page{j}", [P, 4, KVD]) for j in range(2)]
            pageT = [tile(f"pageT{j}", [P, 4 * HALVES, P]) for j in range(2)]
            score = tile("score", [P, NB, PG, NH])
            part = tile("part", [P, NB, PG, NH])
            qbd = tile("qbd", [P, HALVES, NB, HH])
            odec = tile("odec", [P, HALVES, NB, HH])
            small = tile("small", [P, 4, NB * NH])
            pages = tile("pages", [1, NB * NPAGE], I32)
            suffix = at(f"dc_suffix{l}", [P, NB, NPAGE, NH], B)
            logf = at(f"dc_logf{l}", [P, NB, NPAGE, NH], B + 4 * COLS)
            vtail = at(f"dc_vtail{l}", [1, NB, KVD], B + 8 * COLS)
            lnew = at(f"dc_lnew{l}", [P, NB * NH], B + 8 * COLS + 4 * NB * KVD)
            t_ps = [flat(0, 2), flat(2, 4)]

            def queries_of(h):
                g = h // HG
                return g // 2, g % 2, (g % 2) * HG + h % HG

            def page_loop(engine, body):
                with engine.Fori(0, NB // 2) as bb:
                    for u in range(2):
                        body(bb, u)

            s_pt, s_q0, s_q, s_log = sem(f"dk_table_{l}"), sem(f"dk_q_clear_{l}"), sem(f"dk_q_{l}"), sem(f"dk_logf_{l}")
            s_page = [sem(f"dk_page{j}_{l}") for j in range(2)]
            s_turned, s_ca, s_cv = sem(f"dk_turned_{l}"), sem(f"dk_copied_act_{l}"), sem(f"dk_copied_dve_{l}")
            s_sc, s_scc, s_new, s_neg = (sem(f"dk_{n}_{l}") for n in ("scores", "scores_copied", "new_scores", "tail_clear"))
            TURN = 2 * QUADS

            def load_pages(sp, bb, u, cache, sems, free):
                for qd in range(QUADS):
                    n = u * QUADS + qd
                    sp.wait_ge(free, TURN * bb + n + 1)
                    for j in range(4):
                        at_ = (2 * bb + u) * NPAGE + 4 * qd + j
                        pid = sp.value_load(pages[0:1, bass.ds(at_, 1)], min_val=0, max_val=POOL - 1)
                        sp.dma_start(page[n % 2][:, j, :],
                                     cache[l, bass.ds(pid, 1)].rearrange("a t g d -> t (a g d)")).then_inc(sems[n % 2], 16)

            with phase() as block:
                @block.sync
                def _(sp):
                    sp.dma_start(pages[:, :], row(page_table.rearrange("b n -> (b n)"))).then_inc(s_pt, 16)
                    sp.wait_ge(s_pt, 16)
                    page_loop(sp, lambda bb, u: load_pages(sp, bb, u, cache_k, s_page, s_turned))

                if fox:
                    @block.gpsimd
                    def _(pool):
                        pool.wait_ge(s_pt, 16)
                        pool.dma_start(lnew[:, :], row(logf_sample.rearrange("b a h -> (b a h)")).partition_broadcast(P))\
                            .then_inc(s_log, 16)
                        pool.dma_start(vtail[:, :, :].rearrange("p b n -> p (b n)"),
                                       row(v_sample[l].rearrange("b a g d -> (b a g d)"))).then_inc(s_log, 16)
                        with pool.Fori(0, NB * NPAGE) as at_:
                            pid = pool.value_load(pages[0:1, bass.ds(at_, 1)], min_val=0, max_val=POOL - 1)
                            pool.dma_start(logf[:, :, :, :].rearrange("p b n h -> p (b n) h")[:, bass.ds(at_, 1), :]
                                           .rearrange("p a h -> p (a h)"),
                                           cache_logf[bass.ds(pid, 1)].rearrange("a t h -> t (a h)")).then_inc(s_log, 16)
                        pool.wait_ge(s_log, 16 * (NB * NPAGE + 2))

                @block.tensor
                def _(pe):
                    pe.sem_inc(s_turned, 2)
                    pe.wait_ge(s_q, 1)
                    if fox:
                        for b in range(NB):
                            for hf in range(HALVES):
                                last = nc.tensor.matmul(bank[0][0:1, (b * HALVES + hf) * HH:(b * HALVES + hf + 1) * HH],
                                                        kvT[:, hf, SEQ + b:SEQ + b + 1], qbd[:, hf, b, :], start=True, stop=True)
                        last.then_inc(s_new, 1)

                    def turn(bb, n):
                        pe.wait_ge(s_page[n % 2], 64 * (QUADS * bb + n // 2 + 1))
                        if n >= 2:
                            pe.wait_ge(s_ca, TURN * bb + n - 1)
                            pe.wait_ge(s_cv, TURN * bb + n - 1)
                        for j in range(4 * HALVES):
                            last = nc.tensor.transpose(t_ps[n % 2][:, j * P:(j + 1) * P],
                                                       page[n % 2][:, j // HALVES, (j % HALVES) * P:(j % HALVES + 1) * P], ident[:, :])
                        last.then_inc(s_turned, 1)

                    def scores(bb, n):
                        pe.wait_ge(s_ca, TURN * bb + n + 1)
                        pe.wait_ge(s_cv, TURN * bb + n + 1)
                        if n >= 2:
                            pe.wait_ge(s_scc, TURN * bb + n - 1)
                        for j in range(4 * HALVES):
                            q = qbd[:, j % HALVES, bass.ds(2 * bb + n // QUADS, 1), :].rearrange("p a h -> p (a h)")
                            last = nc.tensor.matmul(psum[:, 4 + n % 2, j * HH:(j + 1) * HH], pageT[n % 2][:, j, :], q,
                                                    start=True, stop=True)
                        last.then_inc(s_sc, 1)

                    with pe.Fori(0, NB // 2) as bb:
                        turn(bb, 0)
                        for n in range(TURN):
                            if n + 1 < TURN:
                                turn(bb, n + 1)
                            scores(bb, n)

                @block.scalar
                def _(act):
                    with act.Fori(0, NB // 2) as bb:
                        for n in range(TURN):
                            act.wait_ge(s_turned, TURN * bb + n + 3)
                            if n >= 2:
                                act.wait_ge(s_sc, TURN * bb + n - 1)
                            nc.scalar.activation(pageT[n % 2][:, 0:4, :].rearrange("p j n -> p (j n)"), t_ps[n % 2][:, 0:512],
                                                 ACT.Copy).then_inc(s_ca, 1)

                @block.vector
                def _(dve):
                    nc.vector.memset(qbd[:, :, :, :], 0.0).then_inc(s_q0, 1)
                    if fox:
                        nc.vector.memset(score[:, :, NPAGE, :], NEG).then_inc(s_neg, 1)
                    dve.wait_ge(s_q0, 1)
                    for h in range(NH):
                        hf, side, c = queries_of(h)
                        last = nc.vector.tensor_copy(qbd[side * HALF:(side + 1) * HALF, hf, :, c],
                                                     qT[(h % 2) * HALF:(h % 2 + 1) * HALF, h // 2, SEQ:TOK])
                    last.then_inc(s_q, 1)
                    if fox:
                        dve.wait_ge(s_new, 1)
                        dve.wait_ge(s_neg, 1)
                        nc.vector.tensor_copy(score[0:1, :, NPAGE, :], bank[0][0:1, 0:NB * NH].rearrange("p (b h) -> p b h", b=NB))
                    with dve.Fori(0, NB // 2) as bb:
                        for n in range(TURN):
                            dve.wait_ge(s_turned, TURN * bb + n + 3)
                            if n >= 2:
                                dve.wait_ge(s_sc, TURN * bb + n - 1)
                            nc.vector.tensor_copy(pageT[n % 2][:, 4:8, :].rearrange("p j n -> p (j n)"),
                                                  t_ps[n % 2][:, 512:1024]).then_inc(s_cv, 1)
                            dve.wait_ge(s_sc, TURN * bb + n + 1)
                            qd = n % QUADS
                            nc.vector.tensor_scalar(score[:, bass.ds(2 * bb + n // QUADS, 1), 4 * qd:4 * qd + 4, :]
                                                    .rearrange("p a j h -> p (a j) h"),
                                                    psum[:, 4 + n % 2, 0:4 * NH].rearrange("p (j h) -> p j h", h=NH),
                                                    **MULT1).then_inc(s_scc, 1)

            s_a, s_v, s_p = sem(f"dw_act_{l}"), sem(f"dw_dve_{l}"), sem(f"dw_pe_{l}")
            c_ps, tot_ps = flat(0, 4), flat(4, 8)
            past = score[:, :, 0:NPAGE, :]
            summand = logf if fox else part

            def bnh(ap):
                return ap[:, 0:COLS].rearrange("p (b n h) -> p b n h", b=NB, n=NPAGE)

            with phase() as block:
                @block.scalar
                def _(act):
                    nc.scalar.preload_act_table_set(EXP_LN_SET)
                    if not fox:
                        nc.scalar.activation(part[:, :, :, :], past, ACT.Abs).then_inc(s_a, 1)
                        act.wait_ge(s_a, 1)
                        nc.scalar.activation(part[:, :, :, :], part[:, :, :, :], ACT.Exp, scale=-1.0).then_inc(s_a, 1)
                        act.wait_ge(s_a, 2)
                        nc.scalar.activation(part[:, :, :, :], part[:, :, :, :], ACT.Ln, bias=1.0).then_inc(s_a, 1)
                    act.wait_ge(s_v, NPAGE + (7 if fox else 3))
                    nc.scalar.activation(score[:, :, :, :], score[:, :, :, :], ACT.Exp).then_inc(s_a, 1)

                @block.tensor
                def _(pe):
                    if not fox:
                        pe.wait_ge(s_v, 1)
                    flat_in = summand[:, :, :, :].rearrange("p b n h -> p (b n h)")
                    for tri, out in ((tri_strict if fox else tri_incl, c_ps), (ones, tot_ps)):
                        for c0, c1 in pieces(0, COLS):
                            last = nc.tensor.matmul(out[:, c0:c1], tri[:, :], flat_in[:, c0:c1], start=True, stop=True)
                    last.then_inc(s_p, 1)
                    if fox:
                        pe.wait_ge(s_v, NPAGE + 3)
                        nc.tensor.transpose(psum[:, 0, 0:P], small[:, 0, :], ident[:, :]).then_inc(s_p, 1)
                        pe.wait_ge(s_v, NPAGE + 5)
                        nc.tensor.matmul(psum[:, 1, 0:P], ones[:, :], small[:, 2, :], start=True, stop=True).then_inc(s_p, 1)
                        pe.wait_ge(s_v, NPAGE + 8)
                        nc.tensor.matmul(psum[:, 2, 0:P], ones[:, :], small[:, 0, :], start=True, stop=True).then_inc(s_p, 1)

                @block.vector
                def _(dve):
                    done = [0]

                    def step(ins):
                        done[0] += 1
                        ins.then_inc(s_v, 1)
                        dve.wait_ge(s_v, done[0])

                    if not fox:
                        dve.wait_ge(s_a, 3)
                        step(nc.vector.scalar_tensor_tensor(out=part[:, :, :, :], in0=past, scalar=0.0, in1=part[:, :, :, :],
                                                            op0=ALU.max, op1=ALU.add))
                        step(nc.vector.memset(suffix[:, :, NPAGE - 1, :], 0.0))
                    else:
                        step(nc.vector.tensor_copy(suffix[:, :, NPAGE - 1, :], lnew[:, :].rearrange("p (b h) -> p b h", b=NB)))
                    dve.wait_ge(s_p, 1)
                    total = bnh(tot_ps)
                    for n in range(NPAGE - 2, -1, -1):
                        step(nc.vector.tensor_tensor(suffix[:, :, n, :], total[:, :, n + 1, :], suffix[:, :, n + 1, :], ALU.add))
                    op = ALU.add if fox else ALU.subtract
                    step(nc.vector.tensor_tensor(past, past, suffix[:, :, :, :], op))
                    flat_c = bnh(c_ps)
                    if not fox:
                        step(nc.vector.tensor_tensor(past, past, flat_c, ALU.subtract))
                        assert done[0] == NPAGE + 3
                        return
                    step(nc.vector.tensor_tensor(past, past, flat_c, ALU.add))
                    by_head = score[:, :, :, :].rearrange("p b n h -> p b h n")
                    step(nc.vector.tensor_reduce(small[:, 0, :].rearrange("p (b h) -> p b h", b=NB), by_head, AX.X, ALU.max))
                    dve.wait_ge(s_p, 2)
                    assert done[0] == NPAGE + 3, done
                    step(nc.vector.tensor_reduce(small[:, 1, 0:1], psum[:, 0, 0:P], AX.X, ALU.max))
                    step(nc.vector.tensor_scalar(small[:, 2, :], ident[:, :], small[:, 1, 0:1], None, ALU.mult))
                    dve.wait_ge(s_p, 3)
                    step(nc.vector.tensor_copy(small[:, 3, :], psum[:, 1, 0:P]))
                    top = small[:, 3, :].rearrange("p (b a h) -> p b a h", b=NB, a=1)
                    step(nc.vector.tensor_tensor(score[:, :, :, :], score[:, :, :, :], top.broadcast_to([P, NB, PG, NH]),
                                                 ALU.subtract))
                    assert done[0] == NPAGE + 7
                    dve.wait_ge(s_a, 1)
                    step(nc.vector.tensor_reduce(small[:, 0, :].rearrange("p (b h) -> p b h", b=NB), by_head, AX.X, ALU.add))
                    dve.wait_ge(s_p, 4)
                    step(nc.vector.reciprocal(small[:, 1, :], psum[:, 2, 0:P]))

            s_page = [sem(f"dv_page{j}_{l}") for j in range(2)]
            s_used, s_ov, s_oc, s_tail = (sem(f"dv_{n}_{l}") for n in ("used", "outputs", "copied", "tail"))
            s_od = sem(f"dv_done_{l}")
            with phase() as block:
                @block.sync
                def _(sp):
                    page_loop(sp, lambda bb, u: load_pages(sp, bb, u, cache_v, s_page, s_used))

                @block.tensor
                def _(pe):
                    pe.sem_inc(s_used, 2)
                    if fox:
                        for b in range(NB):
                            for hf in range(HALVES):
                                c = (b * HALVES + hf) * HH
                                last = nc.tensor.matmul(psum[:, 0, c:c + HH], vtail[0:1, b, hf * P:(hf + 1) * P],
                                                        score[0:1, b, NPAGE, hf * HH:(hf + 1) * HH], start=True, stop=True)
                        last.then_inc(s_tail, 1)
                    with pe.Fori(0, NB // 2) as bb:
                        for n in range(TURN):
                            u, qd = n // QUADS, n % QUADS
                            pe.wait_ge(s_page[n % 2], 64 * (QUADS * bb + n // 2 + 1))
                            if qd == 0:
                                pe.wait_ge(s_oc, 2 * bb + u + 1)
                            for j in range(4):
                                for hf in range(HALVES):
                                    w = score[:, bass.ds(2 * bb + u, 1), 4 * qd + j, hf * HH:(hf + 1) * HH]
                                    last = nc.tensor.matmul(psum[:, 4 + 2 * u + hf, 0:HH], page[n % 2][:, j, hf * P:(hf + 1) * P],
                                                            w.rearrange("p a h -> p (a h)"), start=(qd == 0 and j == 0),
                                                            stop=(qd == QUADS - 1 and j == 3))
                            last.then_inc(s_used, 1)

                @block.vector
                def _(dve):
                    dve.sem_inc(s_oc, 2)
                    with dve.Fori(0, NB // 2) as bb:
                        for u in range(2):
                            dve.wait_ge(s_used, TURN * bb + (u + 1) * QUADS + 2)
                            nc.vector.tensor_scalar(odec[:, :, bass.ds(2 * bb + u, 1), :].rearrange("p f a h -> p f (a h)"),
                                                    psum[:, 4 + 2 * u:6 + 2 * u, 0:HH], **MULT1).then_inc(s_oc, 1)
                    dve.wait_ge(s_oc, NB + 2)
                    if fox:
                        dve.wait_ge(s_tail, 1)
                        nc.vector.tensor_tensor(odec[:, :, :, :], psum[:, 0, 0:NB * NH].rearrange("p (b f h) -> p f b h", b=NB, f=HALVES),
                                                odec[:, :, :, :], ALU.add).then_inc(s_od, 1)
                        dve.wait_ge(s_od, 1)
                        rden = small[:, 1, :].rearrange("p (b f h) -> p f b h", b=NB, f=HALVES)
                        nc.vector.tensor_tensor(odec[:, :, :, :], odec[:, :, :, :], rden, ALU.mult).then_inc(s_od, 1)
                        dve.wait_ge(s_od, 2)
                    for h in range(NH):
                        hf, side, c = queries_of(h)
                        nc.vector.tensor_copy(oT[(h % 2) * HALF:(h % 2 + 1) * HALF, h // 2, SEQ:TOK],
                                              odec[side * HALF:(side + 1) * HALF, hf, :, c])

        setup()
        for l in range(DEPTH):
            norm(f"mix{l}", l)
            project_qkv(l)
            if l == 1:
                log_forget()
            kv_rows(l)
            if l == 0:
                stick_prompt()
            else:
                fox_prompt()
            decode(l)
            project_out(l)
            norm(f"ffn{l}", 2 + l)
            ffn_parameters(l)
            ffn(l)
        norm("final", 4, final=True)
        store_y()


_INS = ['x_prompt', 'x_sample', 'cache_k', 'cache_v', 'cache_logf', 'state_conv', 'page_table',
        'norm_mix', 'norm_ffn', 'norm_final', 'w_qkv', 'w_o', 'fox_w_f', 'fox_b_f',
        'ffn_w_a', 'ffn_w_b', 'ffn_conv_w', 'ffn_conv_b', 'ffn_w_down']


def kernel(**inputs):
    import numpy as _np
    import concourse.bacc as _bacc
    from concourse import mybir as _mybir
    from concourse.bass_utils import run_bass_kernel_spmd as _run

    depth, _, _, nkv, dh = inputs['cache_k'].shape
    b, seq, d = inputs['x_prompt'].shape
    nb = inputs['x_sample'].shape[0]
    nh = inputs['cache_logf'].shape[2]
    f = inputs['ffn_w_a'].shape[2]
    outs = [(b, seq, d), (nb, 1, d),
            (depth, b, seq, nkv, dh), (depth, b, seq, nkv, dh), (depth, nb, 1, nkv, dh), (depth, nb, 1, nkv, dh),
            (b, seq, nh), (nb, 1, nh), (depth, b, 2, f), (depth, nb, 2, f)]
    nc = _bacc.Bacc("TRN2", target_bir_lowering=False, num_devices=1)
    arrays, args = {}, []
    for name in _INS:
        a = _np.ascontiguousarray(inputs[name])
        arrays[f"in_{name}_dram"] = a
        args.append(nc.dram_tensor(f"in_{name}_dram", a.shape, _mybir.dt.from_np(a.dtype), kind="ExternalInput").ap())
    for i, shape in enumerate(outs):
        args.append(nc.dram_tensor(f"out_{i}_dram", shape, _mybir.dt.float32, kind="ExternalOutput").ap())
    trunk_program(nc, *args)
    r = _run(nc, [arrays], core_ids=[0])
    got = [r.results[0][f"out_{i}_dram"] for i in range(len(outs))]
    return tuple(got[:8]) + (None, None) + tuple(got[8:])
```

```python
import concourse.bass as bass
from concourse import mybir
from contextlib import ExitStack, contextmanager

F32 = mybir.dt.float32
F32R = mybir.dt.float32r
I32 = mybir.dt.int32
ALU = mybir.AluOpType
ACT = mybir.ActivationFunctionType
AX = mybir.AxisListType
P = 128
HALF = 64
GROUP_COLS = 256
NEG = -1.0e30
RMS_EPS = 1e-6
EXP_LN_SET = "natural_log_exp_and_others"


def trunk_program(nc, x_prompt, x_sample, cache_k, cache_v, cache_logf, state_conv, page_table,
                  norm_mix, norm_ffn, norm_final, w_qkv, w_o, fox_w_f, fox_b_f,
                  ffn_w_a, ffn_w_b, ffn_conv_w, ffn_conv_b, ffn_w_down,
                  y_prompt, y_sample, k_prompt, v_prompt, k_sample, v_sample,
                  logf_prompt, logf_sample, conv_prompt, conv_sample):
    SEQ, D = x_prompt.shape[1], x_prompt.shape[2]
    NB = x_sample.shape[0]
    DEPTH, POOL, PAGE, NKV, DH = cache_k.shape
    NPAGE = page_table.shape[1]
    NH = D // DH
    HG = NH // NKV
    KVD = NKV * DH
    F = ffn_w_a.shape[2]
    TOK = SEQ + NB
    KT = D // P
    ST = SEQ // P
    CG = 3
    NG = TOK // CG
    FT = F // P
    CHUNKS = F // GROUP_COLS
    NPAR = 2 * NB + 4
    SCALE = float(DH) ** -0.5
    assert TOK % (2 * CG) == 0 and NG <= 512 and DH == HALF and PAGE == P and NKV == 4 and HG == 4
    assert F % GROUP_COLS == 0 and SEQ % P == 0

    ctx = ExitStack()
    with ctx:
        base = ctx.enter_context(nc.sbuf_tensor("arena", [P, (nc.sbuf_usable_end - nc.sbuf_base - 256) // 4], F32))
        start = nc.sbuf_base - 4 * base.shape[1]
        start += -start % 32
        room = 4 * base.shape[1] - 32
        TILE = TOK * 4
        KTILES = KT * TILE
        RAW = KT * GROUP_COLS * 4
        X, A, B, C = start, start + KTILES, start + 2 * KTILES, start + 3 * KTILES
        DD = start + 4 * KTILES
        W = DD + 4 * TILE
        WBYTES = 7 * RAW
        CONST = W + WBYTES

        def at(name, shape, off, dt=F32):
            return nc.alloc_sbuf_tensor_at(name, shape, dt, offset=off)

        pos = [CONST]

        def const(name, shape, dt=F32):
            n = 4
            for s in shape[1:]:
                n *= s
            off = pos[0]
            pos[0] += n + (-n % 32)
            assert pos[0] <= start + room, (name, pos[0] - start, room)
            return at(name, shape, off, dt)

        ident = const("ident", [P, P])
        tri_incl = const("tri_incl", [P, P])
        tri_comp = const("tri_comp", [P, P])
        tri_strict = const("tri_strict", [P, P])
        ones = const("ones", [P, P])
        causal = const("causal", [P, P])
        gain = const("gain", [P, KT, 5])
        fpar = const("fpar", [P, FT, NPAR])
        fcur = const("fcur", [P, 2, NPAR])
        xT = at("xT", [P, KT, TOK], X)
        h_hi = at("h_hi", [P, KT, TOK], A, F32R)
        h_lo = at("h_lo", [P, KT, TOK], B, F32R)
        raw = at("raw", [P, KT, GROUP_COLS], W)
        w_hi = [at(f"w_hi{s}", [P, KT, GROUP_COLS], W + RAW * (1 + 2 * s), F32R) for s in range(3)]
        w_lo = [at(f"w_lo{s}", [P, KT, GROUP_COLS], W + RAW * (2 + 2 * s), F32R) for s in range(3)]
        qkvT = at("qkvT", [P, KT + 4, TOK], C)
        qT = qkvT[:, 0:KT, :]
        kvT = qkvT[:, KT:KT + 4, :]
        oT = at("oT", [P, KT, TOK], A)
        o_hi = at("o_hi", [P, KT, TOK], B, F32R)
        o_lo = at("o_lo", [P, KT, TOK], C, F32R)

        psum = ctx.enter_context(nc.psum_tensor("psum", [P, 8, 512], F32))
        acc = [psum[:, 3 * s:3 * s + 3, :] for s in range(2)]
        bank = [psum[:, 6 + b, :] for b in range(2)]

        def flat(b0, b1):
            return psum[:, b0:b1, :].rearrange("p b n -> p (b n)")

        ncum_dram = nc.dram_tensor("ncum_scratch", [NH, SEQ], F32, kind="Internal").ap()

        mine, before = [], []

        def sem(name):
            guard = nc.semaphore(name)
            mine.append((guard, guard.__enter__()))
            return mine[-1][1]

        s_pool_page = [ctx.enter_context(nc.semaphore(f"pool_page{j}")) for j in range(2)]
        s_pool_load = ctx.enter_context(nc.semaphore("pool_load"))

        shared = []

        @contextmanager
        def phase():
            if shared:
                yield shared[-1]
                return
            with nc.Block() as block:
                @block.sync
                def _(sp):
                    for _, s in before:
                        sp.sem_clear(s)
                yield block
            for guard, _ in before:
                guard.__exit__(None, None, None)
            before[:] = mine
            mine.clear()

        @contextmanager
        def together():
            with phase() as block:
                shared.append(block)
                yield
                shared.pop()

        def row(ap1d):
            return ap1d.rearrange("(a n) -> a n", a=1)

        def setup():
            xrow = at("xrow", [P, ST, D], A)
            xs_row = at("xs_row", [NB, D], B)
            nrow = at("nrow", [5, D], B + D * 4)
            loaded = sem("setup_loaded")
            s_id0, s_id = sem("setup_memset"), sem("setup_const")
            s_t, s_e, s_g = sem("setup_transposed"), sem("setup_evacuated"), sem("setup_gain")
            with phase() as block:
                @block.sync
                def _(sp):
                    for i in range(ST):
                        sp.dma_start(xrow[:, i, :], x_prompt[0, i * P:(i + 1) * P, :]).then_inc(loaded, 16)
                    sp.dma_start(xs_row[:, :], x_sample[:, 0, :]).then_inc(loaded, 16)
                    for n, r in enumerate((norm_mix[0], norm_mix[1], norm_ffn[0], norm_ffn[1], norm_final)):
                        sp.dma_start(nrow[n:n + 1, :], row(r)).then_inc(loaded, 16)

                @block.gpsimd
                def _(pool):
                    for t, v in ((ident, 0.0), (tri_incl, 1.0), (tri_comp, 1.0), (tri_strict, 1.0),
                                 (ones, 1.0), (causal, 0.0)):
                        nc.gpsimd.memset(t[:, :], v).then_inc(s_id0, 1)
                    pool.wait_ge(s_id0, 6)
                    for t, op, fill, b0, step, mul in (
                            (ident, ALU.not_equal, 1.0, 0, -1, 1),
                            (tri_incl, ALU.is_ge, 0.0, 0, -1, 1),
                            (tri_comp, ALU.is_ge, 0.0, -1, 1, -1),
                            (tri_strict, ALU.is_ge, 0.0, -1, -1, 1),
                            (causal, ALU.is_ge, NEG, 0, -1, 1)):
                        nc.gpsimd.affine_select(out=t[:, :], in_=t[:, :], compare_op=op, fill=fill, base=b0,
                                                pattern=[[step, P]], channel_multiplier=mul).then_inc(s_id, 1)

                @block.tensor
                def _(pe):
                    pe.wait_ge(s_id, 5)
                    pe.wait_ge(loaded, 16 * (ST + 6))
                    for c in range(KT):
                        if c >= 2:
                            pe.wait_ge(s_e, c - 1)
                        for i in range(ST):
                            nc.tensor.transpose(acc[c % 2][:, i // 4, (i % 4) * P:(i % 4 + 1) * P],
                                                xrow[:, i, c * P:(c + 1) * P], ident[:, :])
                        nc.tensor.transpose(acc[c % 2][:, 2, 0:NB], xs_row[:, c * P:(c + 1) * P],
                                            ident[0:NB, 0:NB])
                        nc.tensor.transpose(acc[c % 2][:, 2, 64:69], nrow[:, c * P:(c + 1) * P],
                                            ident[0:5, 0:5]).then_inc(s_t, 1)

                @block.vector
                def _(dve):
                    for c in range(KT):
                        dve.wait_ge(s_t, c + 1)
                        for b0 in range(0, ST, 4):
                            n = min(4, ST - b0) * P
                            nc.vector.tensor_copy(xT[:, c, b0 * P:b0 * P + n], acc[c % 2][:, b0 // 4, 0:n])
                        nc.vector.tensor_copy(gain[:, c, :], acc[c % 2][:, 2, 64:69])
                        nc.vector.tensor_copy(xT[:, c, SEQ:TOK], acc[c % 2][:, 2, 0:NB]).then_inc(s_e, 1)

        def norm(tag, g, final=False):
            sq = [at(f"sq{s}_{tag}", [P, TOK], C + s * TILE) for s in range(2)]
            total = at(f"total_{tag}", [P, TOK], C + 2 * TILE)
            rstd = at(f"rstd_{tag}", [P, TOK], C + 3 * TILE)
            var = sq[1]
            full = [sq[0], sq[1], total, at(f"full_{tag}", [P, TOK], DD)]
            NF = len(full)
            s_sq, s_add, s_mm, s_var = sem(f"sq_{tag}"), sem(f"add_{tag}"), sem(f"sum_{tag}"), sem(f"var_{tag}")
            s_std, s_r, s_full, s_hi, s_lo = (sem(f"{n}_{tag}") for n in ("std", "rstd", "full", "hi", "lo"))
            s_lo_odd = sem(f"lo_odd_{tag}")
            with phase() as block:
                @block.scalar
                def _(act):
                    for k in range(KT):
                        if k >= 3:
                            act.wait_ge(s_add, k - 2)
                        nc.scalar.activation((total if k == 0 else sq[k % 2])[:, :], xT[:, k, :], ACT.Square).then_inc(s_sq, 1)
                    act.wait_ge(s_var, 1)
                    nc.scalar.activation(rstd[:, :], var[:, :], ACT.Sqrt).then_inc(s_std, 1)
                    if final:
                        return
                    for k in range(KT):
                        act.wait_ge(s_full, k + 1)
                        nc.scalar.activation(h_hi[:, k, :], full[k % NF][:, :], ACT.Copy).then_inc(s_hi, 1)

                @block.tensor
                def _(pe):
                    pe.wait_ge(s_add, KT - 1)
                    for c in range(CG):
                        last = nc.tensor.matmul(acc[0][:, c, 0:NG], ones[:, :], total[:, c * NG:(c + 1) * NG],
                                                start=True, stop=True)
                    last.then_inc(s_mm, 1)

                @block.vector
                def _(dve):
                    for k in range(1, KT):
                        dve.wait_ge(s_sq, k + 1)
                        if k >= 2:
                            dve.wait_ge(s_add, k - 1)
                        nc.vector.tensor_tensor(total[:, :], total[:, :], sq[k % 2][:, :], ALU.add).then_inc(s_add, 1)
                    dve.wait_ge(s_mm, 1)
                    nc.vector.tensor_scalar(var[:, :].rearrange("p (c n) -> p c n", c=CG), acc[0][:, :, 0:NG],
                                            1.0 / D, RMS_EPS, ALU.mult, ALU.add).then_inc(s_var, 1)
                    dve.wait_ge(s_std, 1)
                    nc.vector.reciprocal(rstd[:, :], rstd[:, :]).then_inc(s_r, 1)
                    dve.wait_ge(s_r, 1)

                    def low_part(k):
                        dve.wait_ge(s_hi, k + 1)
                        nc.vector.tensor_tensor(h_lo[:, k, :], full[k % NF][:, :], h_hi[:, k, :].bitcast(F32),
                                                ALU.subtract).then_inc(s_lo_odd, 1)

                    for k in range(KT):
                        if k >= NF and not final:
                            if k % 2 == 0:
                                dve.wait_ge(s_lo, (k - NF) // 2 + 1)
                            else:
                                dve.wait_ge(s_lo_odd, (k - NF) // 2 + 1)
                        out = xT[:, k, :] if final else full[k % NF][:, :]
                        nc.vector.scalar_tensor_tensor(out=out, in0=xT[:, k, :], scalar=gain[:, k, g:g + 1],
                                                       in1=rstd[:, :], op0=ALU.mult, op1=ALU.mult).then_inc(s_full, 1)
                        if k % 2 == 0 and k >= 2 and not final:
                            low_part(k - 1)
                    if not final:
                        low_part(KT - 1)

                @block.gpsimd
                def _(pool):
                    if final:
                        return
                    for k in range(0, KT, 2):
                        pool.wait_ge(s_hi, k + 1)
                        nc.gpsimd.tensor_tensor(h_lo[:, k, :], full[k % NF][:, :], h_hi[:, k, :].bitcast(F32),
                                                ALU.subtract).then_inc(s_lo, 1)

            def tile_ready(engine, k):
                engine.wait_ge(s_lo_odd if k % 2 else s_lo, k // 2 + 1)

            return tile_ready

        def split_product(out, hi, lo, cols, rhs_hi, rhs_lo, kt, pe=None, tile_ready=None):
            for k in range(kt):
                if tile_ready is not None:
                    tile_ready(pe, k)
                for part, (w, r) in enumerate(((hi, rhs_hi), (hi, rhs_lo), (lo, rhs_hi))):
                    for c in range(CG):
                        last = nc.tensor.matmul(out[:, c, 0:NG], w[:, k, cols], r[:, k, c * NG:(c + 1) * NG],
                                                start=(k == 0 and part == 0), stop=(k == kt - 1 and part == 2))
            return last

        def gemm(tag, turns, weights, rhs_hi, rhs_lo, evacuate, source=None, tile_ready=None):
            s_w, s_hi, s_lo = sem(f"w_loaded_{tag}"), sem(f"w_hi_{tag}"), sem(f"w_lo_{tag}")
            s_slot, s_acc, s_free = sem(f"slot_used_{tag}"), sem(f"acc_ready_{tag}"), sem(f"acc_free_{tag}")
            s_rhi, s_rlo = sem(f"rhs_hi_{tag}"), sem(f"rhs_lo_{tag}")
            with phase() as block:
                @block.sync
                def _(sp):
                    with sp.Fori(0, turns) as i:
                        for u in range(2):
                            sp.wait_ge(s_lo, 2 * i + u + 1)
                            sp.dma_start(raw[:, :, :], weights(i, u)).then_inc(s_w, 16)

                @block.scalar
                def _(act):
                    if source is not None:
                        for k in range(KT):
                            nc.scalar.activation(rhs_hi[:, k, :], source[:, k, :], ACT.Copy).then_inc(s_rhi, 1)
                    with act.Fori(0, turns) as i:
                        for u in range(2):
                            act.wait_ge(s_w, 32 * i + 16 * (u + 1))
                            act.wait_ge(s_slot, 2 * i + u + 1)
                            nc.scalar.activation(w_hi[u][:, :, :], raw[:, :, :], ACT.Copy).then_inc(s_hi, 1)

                @block.gpsimd
                def _(pool):
                    pool.sem_inc(s_lo, 1)
                    with pool.Fori(0, turns) as i:
                        for u in range(2):
                            pool.wait_ge(s_hi, 2 * i + u + 1)
                            nc.gpsimd.tensor_tensor(w_lo[u][:, :, :], raw[:, :, :], w_hi[u][:, :, :].bitcast(F32),
                                                    ALU.subtract).then_inc(s_lo, 1)

                @block.tensor
                def _(pe):
                    pe.sem_inc(s_slot, 2)
                    if source is not None:
                        pe.wait_ge(s_rlo, KT)
                    with pe.Fori(0, turns) as i:
                        for u in range(2):
                            pe.wait_ge(s_lo, 2 * i + u + 2)
                            for m in range(2):
                                pe.wait_ge(s_free, 4 * i + 2 * u + m + 1)
                                split_product(acc[m], w_hi[u], w_lo[u], slice(m * P, (m + 1) * P), rhs_hi, rhs_lo, KT,
                                              pe, tile_ready if u == 0 and m == 0 else None).then_inc(s_acc, 1)
                            pe.wait_ge(s_acc, 4 * i + 2 * u + 2)
                            pe.sem_inc(s_slot, 1)

                @block.vector
                def _(dve):
                    if source is not None:
                        for k in range(KT):
                            dve.wait_ge(s_rhi, k + 1)
                            nc.vector.tensor_tensor(rhs_lo[:, k, :], source[:, k, :], rhs_hi[:, k, :].bitcast(F32),
                                                    ALU.subtract).then_inc(s_rlo, 1)
                    dve.sem_inc(s_free, 2)
                    with dve.Fori(0, turns) as i:
                        for tile in range(4):
                            dve.wait_ge(s_acc, 4 * i + tile + 1)
                            evacuate(i, tile).then_inc(s_free, 1)

        def cols3(ap):
            return ap.rearrange("p a (c n) -> p (a c) n", c=CG)

        def project_qkv(l, tile_ready):
            view = w_qkv[l].rearrange("(k p) (t u n) -> p k t u n", p=P, u=2, n=GROUP_COLS)
            gemm(f"qkv{l}", (D + 2 * KVD) // (2 * GROUP_COLS),
                 lambda i, u: view[:, :, bass.ds(i, 1), u, :].rearrange("p k t n -> p k (t n)"), h_hi, h_lo,
                 lambda i, tile: nc.vector.tensor_scalar(cols3(qkvT[:, bass.ds(4 * i + tile, 1), :]),
                                                         acc[tile % 2][:, :, 0:NG], 1.0, None, ALU.mult), tile_ready=tile_ready)

        tokv = at("tokv", [P, ST + 1, KVD], W)
        tokk = at("tokk", [P, ST + 1, KVD], W + WBYTES - (ST + 1) * KVD * 4)

        def kv_rows(l, ready=()):
            s_t, s_e, s_out = sem(f"kv_turned_{l}"), sem(f"kv_rows_{l}"), sem(f"kv_stored_{l}")
            with phase() as block:
                @block.tensor
                def _(pe):
                    for s, n in ready:
                        pe.wait_ge(s, n)
                    for i in range(ST + 1):
                        n = P if i < ST else NB
                        if i >= 2:
                            pe.wait_ge(s_e, i - 1)
                        for t in range(4):
                            last = nc.tensor.transpose(bank[i % 2][0:n, t * P:(t + 1) * P], kvT[:, t, i * P:i * P + n],
                                                       ident[:, :])
                        last.then_inc(s_t, 1)

                @block.vector
                def _(dve):
                    for i in range(ST + 1):
                        n = P if i < ST else NB
                        dve.wait_ge(s_t, i + 1)
                        nc.vector.tensor_copy(tokk[0:n, i, :], bank[i % 2][0:n, 0:KVD])
                        nc.vector.tensor_copy(tokv[0:n, i, :], bank[i % 2][0:n, KVD:2 * KVD]).then_inc(s_e, 1)

                @block.sync
                def _(sp):
                    for i in range(ST + 1):
                        sp.wait_ge(s_e, i + 1)
                        for rows, outs in ((tokk, (k_prompt, k_sample)), (tokv, (v_prompt, v_sample))):
                            if i < ST:
                                dst = outs[0][l, 0, i * P:(i + 1) * P].rearrange("t g d -> t (g d)")
                                src = rows[:, i, :]
                            else:
                                dst = outs[1][l, :, 0].rearrange("b g d -> b (g d)")
                                src = rows[0:NB, ST, :]
                            sp.dma_start(dst, src).then_inc(s_out, 16)
                    sp.wait_ge(s_out, 32 * (ST + 1))

        def project_out(l):
            view = w_o[l].rearrange("(k p) (t u n) -> p k t u n", p=P, u=2, n=GROUP_COLS)
            gemm(f"o{l}", D // (2 * GROUP_COLS),
                 lambda i, u: view[:, :, bass.ds(i, 1), u, :].rearrange("p k t n -> p k (t n)"), o_hi, o_lo,
                 lambda i, tile: nc.vector.tensor_tensor(cols3(xT[:, bass.ds(4 * i + tile, 1), :]), acc[tile % 2][:, :, 0:NG],
                                                         cols3(xT[:, bass.ds(4 * i + tile, 1), :]), ALU.add),
                 source=oT)

        def ffn_parameters(l):
            prow = at(f"prow{l}", [NPAR, F], C + 4 * TILE)
            s_in, s_t, s_e = sem(f"par_loaded_{l}"), sem(f"par_turned_{l}"), sem(f"par_copied_{l}")
            per_bank = 512 // NPAR
            with phase() as block:
                @block.sync
                def _(sp):
                    sp.dma_start(prow[0:2 * NB, :], state_conv[l].rearrange("b j f -> (b j) f")).then_inc(s_in, 16)
                    sp.dma_start(prow[2 * NB:2 * NB + 3, :], ffn_conv_w[l]).then_inc(s_in, 16)
                    sp.dma_start(prow[2 * NB + 3:NPAR, :], row(ffn_conv_b[l])).then_inc(s_in, 16)
                    sp.dma_start(conv_sample[l, :, 0, :], state_conv[l, :, 1, :]).then_inc(s_in, 16)
                    sp.wait_ge(s_in, 64)

                @block.tensor
                def _(pe):
                    pe.wait_ge(s_in, 64)
                    for f in range(FT):
                        last = nc.tensor.transpose(bank[f // per_bank][:, (f % per_bank) * NPAR:(f % per_bank + 1) * NPAR],
                                                   prow[:, f * P:(f + 1) * P], ident[0:NPAR, 0:NPAR])
                    last.then_inc(s_t, 1)

                @block.vector
                def _(dve):
                    dve.wait_ge(s_t, 1)
                    for b0 in range(0, FT, per_bank):
                        n = min(per_bank, FT - b0)
                        nc.vector.tensor_copy(fpar[:, b0:b0 + n, :].rearrange("p f r -> p (f r)"),
                                              bank[b0 // per_bank][:, 0:n * NPAR]).then_inc(s_e, 1)
            return ((s_e, -(-FT // per_bank)),)

        act_hi = at("act_hi", [P, 2, TOK], C, F32R)
        act_lo = at("act_lo", [P, 2, TOK], C + 2 * TILE, F32R)
        conv = [at(f"conv{m}", [P, TOK], C + (4 + m) * TILE) for m in range(2)]
        gate = [at(f"gate{m}", [P, TOK], C + (6 + m) * TILE) for m in range(2)]
        a_pad = [at(f"a_pad{m}", [P, TOK + 2], DD + m * (TILE + 32)) for m in range(2)]
        conv_rows = at("conv_rows", [P, 2, P], DD + 2 * (TILE + 32))

        def ffn(l, tile_ready, par_ready):
            s_w, s_hi, s_lo = sem(f"ffn_w_loaded_{l}"), sem(f"ffn_w_hi_{l}"), sem(f"ffn_w_lo_{l}")
            s_a, s_b, s_down = sem(f"ffn_a_ready_{l}"), sem(f"ffn_b_ready_{l}"), sem(f"ffn_down_ready_{l}")
            s_acopy, s_gated, s_added = sem(f"ffn_a_copied_{l}"), sem(f"ffn_gated_{l}"), sem(f"ffn_added_{l}")
            s_tap, s_c1, s_conv, s_gelu = (sem(f"ffn_{n}_{l}") for n in ("tap2", "tap1", "conv", "gelu"))
            s_ahi, s_alo = sem(f"ffn_act_hi_{l}"), sem(f"ffn_act_lo_{l}")
            s_par, s_rt, s_rc = sem(f"ffn_par_{l}"), sem(f"ffn_rows_turned_{l}"), sem(f"ffn_rows_copied_{l}")
            s_out = [sem(f"ffn_rows_stored{m}_{l}") for m in range(2)]
            up = [w[l].rearrange("(k p) (i n) -> p k i n", p=P, n=GROUP_COLS) for w in (ffn_w_a, ffn_w_b)]
            down = ffn_w_down[l].rearrange("(i k p) n -> p i k n", k=2, p=P)
            state_p = conv_prompt[l, 0].rearrange("j (t n) -> j t n", n=P)
            state_s = conv_sample[l, :, 1, :].rearrange("b (t n) -> b t n", n=P)

            def as_down(t):
                return t[:, :, :].rearrange("p k n -> p (k n)").rearrange("p (k n) -> p k n", k=2)

            raw_down, down_hi, down_lo = as_down(raw), as_down(w_hi[2]), as_down(w_lo[2])
            END = CHUNKS - 1
            assert CHUNKS >= 2

            def over_chunks(engine, body):
                body(0, True, False)
                if CHUNKS > 2:
                    with engine.Fori(1, END) as i:
                        body(i, False, False)
                body(END, False, True)

            def number_down(i, last):
                return 3 * i + 2 if last else 3 * i + 3

            with phase() as block:
                @block.sync
                def _(sp):
                    def load(dst, src, n):
                        sp.wait_ge(s_lo, n + 1)
                        sp.dma_start(dst, src).then_inc(s_w, 16)

                    def load_up(u, i, n):
                        load(raw[:, :, :], up[u][:, :, bass.ds(i, 1), :].rearrange("p k t n -> p k (t n)"), n)

                    load_up(0, 0, 0)
                    load_up(1, 0, 1)

                    def body(i, first, last):
                        if not last:
                            load_up(0, i + 1, 3 * i + 2)
                        load(raw_down, down[:, bass.ds(i, 1), :, :].rearrange("p i k n -> p (i k) n"),
                             number_down(i, last))
                        if not last:
                            load_up(1, i + 1, 3 * i + 4)
                        for m in range(2):
                            sp.wait_ge(s_rc, 2 * i + m + 1)
                            sp.dma_start(state_p[:, bass.ds(2 * i + m, 1), :].rearrange("j t n -> j (t n)"),
                                         conv_rows[P - 2 - NB:P - NB, m, :]).then_inc(s_out[m], 16)
                            sp.dma_start(state_s[:, bass.ds(2 * i + m, 1), :].rearrange("j t n -> j (t n)"),
                                         conv_rows[P - NB:P, m, :]).then_inc(s_out[m], 16)

                    over_chunks(sp, body)
                    for m in range(2):
                        sp.wait_ge(s_out[m], 32 * CHUNKS)

                @block.scalar
                def _(act):
                    def hi_part(dst, src, n):
                        act.wait_ge(s_w, 16 * n + 16)
                        nc.scalar.activation(dst, src, ACT.Copy).then_inc(s_hi, 1)

                    for u in range(2):
                        hi_part(w_hi[u][:, :, :], raw[:, :, :], u)

                    def body(i, first, last):
                        for m in range(2):
                            act.wait_ge(s_a, 2 * i + m + 1)
                            if not first:
                                act.wait_ge(s_rt, 2 * i + m - 1)
                            nc.scalar.activation(a_pad[m][:, 2:2 + TOK].rearrange("p (c n) -> p c n", c=CG),
                                                 acc[0][:, :, 0:NG], ACT.Copy).then_inc(s_acopy, 1)
                            if m == 0 and not first:
                                hi_part(w_hi[1][:, :, :], raw[:, :, :], 3 * i + 1)
                            if m == 1 and not last:
                                hi_part(w_hi[0][:, :, :], raw[:, :, :], 3 * i + 2)
                            act.wait_ge(s_par, i + 1)
                            act.wait_ge(s_acopy, 2 * i + m + 1)
                            nc.scalar.activation(conv[m][:, :], a_pad[m][:, 2:2 + TOK], ACT.Identity,
                                                 scale=fcur[:, m, 2 * NB + 2:2 * NB + 3],
                                                 bias=fcur[:, m, 2 * NB + 3:NPAR]).then_inc(s_tap, 1)
                            act.wait_ge(s_conv, 2 * i + m + 1)
                            nc.scalar.activation(conv[m][:, :], conv[m][:, :], ACT.Gelu_apprx_tanh).then_inc(s_gelu, 1)
                            act.wait_ge(s_gated, 2 * i + m + 1)
                            nc.scalar.activation(act_hi[:, m, :], gate[m][:, :], ACT.Copy).then_inc(s_ahi, 1)
                        hi_part(down_hi, raw_down, number_down(i, last))

                    over_chunks(act, body)

                @block.gpsimd
                def _(pool):
                    pool.sem_inc(s_lo, 1)

                    def lo_part(dst, src, hi, n):
                        pool.wait_ge(s_hi, n + 1)
                        nc.gpsimd.tensor_tensor(dst, src, hi, ALU.subtract).then_inc(s_lo, 1)

                    for u in range(2):
                        lo_part(w_lo[u][:, :, :], raw[:, :, :], w_hi[u][:, :, :].bitcast(F32), u)

                    def body(i, first, last):
                        for m in range(2):
                            if m == 0 and not first:
                                lo_part(w_lo[1][:, :, :], raw[:, :, :], w_hi[1][:, :, :].bitcast(F32), 3 * i + 1)
                            if m == 1 and not last:
                                lo_part(w_lo[0][:, :, :], raw[:, :, :], w_hi[0][:, :, :].bitcast(F32), 3 * i + 2)
                            pool.wait_ge(s_ahi, 2 * i + m + 1)
                            nc.gpsimd.tensor_tensor(act_lo[:, m, :], gate[m][:, :], act_hi[:, m, :].bitcast(F32),
                                                    ALU.subtract).then_inc(s_alo, 1)
                        lo_part(down_lo, raw_down, down_hi.bitcast(F32), number_down(i, last))

                    over_chunks(pool, body)

                @block.vector
                def _(dve):
                    def add_down(i):
                        for t in range(KT):
                            dve.wait_ge(s_down, KT * i + t + 1)
                            side = t % 2 if isinstance(i, int) and i == END else (t + 1) % 2
                            nc.vector.tensor_tensor(cols3(xT[:, t:t + 1, :]), acc[side][:, :, 0:NG], cols3(xT[:, t:t + 1, :]),
                                                    ALU.add).then_inc(s_added, 1)

                    def body(i, first, last):
                        nc.vector.tensor_copy(fcur[:, :, :], fpar[:, bass.ds(2 * i, 2), :]).then_inc(s_par, 1)
                        if not first:
                            add_down(i - 1)
                        for m in range(2):
                            def tap(j):
                                return fcur[:, m, 2 * NB + j:2 * NB + j + 1]
                            state = fcur[:, m, 0:2 * NB].rearrange("p (b j) -> p j b", j=2)
                            dve.wait_ge(s_par, i + 1)
                            dve.wait_ge(s_tap, 2 * i + m + 1)
                            nc.vector.scalar_tensor_tensor(out=conv[m][:, 0:SEQ], in0=a_pad[m][:, 1:1 + SEQ], scalar=tap(1),
                                                           in1=conv[m][:, 0:SEQ], op0=ALU.mult, op1=ALU.add)
                            nc.vector.scalar_tensor_tensor(out=conv[m][:, SEQ:TOK], in0=state[:, 1, :], scalar=tap(1),
                                                           in1=conv[m][:, SEQ:TOK], op0=ALU.mult, op1=ALU.add).then_inc(s_c1, 1)
                            dve.wait_ge(s_c1, 2 * i + m + 1)
                            nc.vector.scalar_tensor_tensor(out=conv[m][:, SEQ:TOK], in0=state[:, 0, :], scalar=tap(0),
                                                           in1=conv[m][:, SEQ:TOK], op0=ALU.mult, op1=ALU.add)
                            nc.vector.scalar_tensor_tensor(out=conv[m][:, 0:SEQ], in0=a_pad[m][:, 0:SEQ], scalar=tap(0),
                                                           in1=conv[m][:, 0:SEQ], op0=ALU.mult, op1=ALU.add).then_inc(s_conv, 1)
                            dve.wait_ge(s_b, 2 * i + m + 1)
                            dve.wait_ge(s_gelu, 2 * i + m + 1)
                            if not first:
                                dve.wait_ge(s_alo, 2 * i + m - 1)
                            nc.vector.tensor_tensor(gate[m][:, :].rearrange("p (c n) -> p c n", c=CG), acc[1][:, :, 0:NG],
                                                    conv[m][:, :].rearrange("p (c n) -> p c n", c=CG),
                                                    ALU.mult).then_inc(s_gated, 1)
                            dve.wait_ge(s_rt, 2 * i + m + 1)
                            if not first:
                                dve.wait_ge(s_out[m], 32 * i)
                            nc.vector.tensor_copy(conv_rows[:, m, :], bank[m][:, 0:P]).then_inc(s_rc, 1)

                    for s, n in par_ready:
                        dve.wait_ge(s, n)
                    for m in range(2):
                        nc.vector.memset(a_pad[m][:, 0:2], 0.0)
                    over_chunks(dve, body)
                    add_down(END)

                @block.tensor
                def _(pe):
                    def down_products(i, last):
                        pe.wait_ge(s_lo, number_down(i, last) + 2)
                        pe.wait_ge(s_alo, 2 * i + 2)
                        for t in range(KT):
                            if t >= 2:
                                pe.wait_ge(s_added, KT * i + t - 1)
                            elif (t == 0) == last:
                                pe.wait_ge(s_acopy, 2 * i + 2 if last else 2 * i + 3)
                            else:
                                pe.wait_ge(s_gated, 2 * i + 2)
                            side = t % 2 if last else (t + 1) % 2
                            split_product(acc[side], down_hi, down_lo, slice(t * P, (t + 1) * P),
                                          act_hi, act_lo, 2).then_inc(s_down, 1)

                    def rows(i, m, first):
                        pe.wait_ge(s_acopy, 2 * i + m + 1)
                        if first:
                            for s, n in par_ready:
                                pe.wait_ge(s, n)
                        else:
                            pe.wait_ge(s_rc, 2 * i + m - 1)
                        nc.tensor.transpose(bank[m][:, 0:P], a_pad[m][:, 2 + TOK - P:2 + TOK], ident[:, :]).then_inc(s_rt, 1)

                    def body(i, first, last):
                        pe.wait_ge(s_lo, 2 if first else 3 * i + 1)
                        if not first:
                            pe.wait_ge(s_acopy, 2 * i)
                        split_product(acc[0], w_hi[0], w_lo[0], slice(0, P), h_hi, h_lo, KT,
                                      pe, tile_ready if first else None).then_inc(s_a, 1)
                        if not first:
                            down_products(i - 1, False)
                            pe.wait_ge(s_added, KT * i - 1)
                        rows(i, 0, first)
                        pe.wait_ge(s_lo, 3 if first else 3 * i + 3)
                        split_product(acc[1], w_hi[1], w_lo[1], slice(0, P), h_hi, h_lo, KT).then_inc(s_b, 1)
                        if not first:
                            pe.wait_ge(s_added, KT * i)
                        pe.wait_ge(s_acopy, 2 * i + 1)
                        split_product(acc[0], w_hi[0], w_lo[0], slice(P, 2 * P), h_hi, h_lo, KT).then_inc(s_a, 1)
                        pe.wait_ge(s_gated, 2 * i + 1)
                        split_product(acc[1], w_hi[1], w_lo[1], slice(P, 2 * P), h_hi, h_lo, KT).then_inc(s_b, 1)
                        rows(i, 1, first)

                    over_chunks(pe, body)
                    down_products(END, True)

        def store_y():
            yrow = at("yrow", [P, 2, D], A)
            s_t, s_e = sem("y_turned"), sem("y_copied")
            s_out = [sem(f"y_stored{u}") for u in range(2)]
            with phase() as block:
                @block.tensor
                def _(pe):
                    for i in range(ST + 1):
                        n = P if i < ST else NB
                        if i >= 2:
                            pe.wait_ge(s_e, i - 1)
                        for c in range(KT):
                            last = nc.tensor.transpose(acc[i % 2][0:n, c // 4, (c % 4) * P:(c % 4 + 1) * P],
                                                       xT[:, c, i * P:i * P + n], ident[:, :])
                        last.then_inc(s_t, 1)

                @block.vector
                def _(dve):
                    for i in range(ST + 1):
                        n = P if i < ST else NB
                        dve.wait_ge(s_t, i + 1)
                        if i >= 2:
                            dve.wait_ge(s_out[i % 2], 16 * (i // 2))
                        nc.vector.tensor_copy(yrow[0:n, i % 2, :].rearrange("p (c n) -> p c n", c=2),
                                              acc[i % 2][0:n, 0:2, :]).then_inc(s_e, 1)

                @block.sync
                def _(sp):
                    for i in range(ST + 1):
                        sp.wait_ge(s_e, i + 1)
                        if i < ST:
                            sp.dma_start(y_prompt[0, i * P:(i + 1) * P, :], yrow[:, i % 2, :]).then_inc(s_out[i % 2], 16)
                        else:
                            sp.dma_start(y_sample[:, 0, :], yrow[0:NB, i % 2, :]).then_inc(s_out[i % 2], 16)
                    for u in range(2):
                        sp.wait_ge(s_out[u], 16 * ((ST + 2 - u) // 2))

        def log_forget():
            TW = W + (ST + 1) * KVD * 4
            wf = at("wf", [P, KT, NH], TW)
            wf_hi = at("wf_hi", [P, KT, P], TW + KT * NH * 4, F32R)
            wf_lo = at("wf_lo", [P, KT, P], TW + KT * (NH + P) * 4, F32R)
            t0 = TW + KT * (NH + 2 * P) * 4
            zb, e, cum, one = (at(f"lf_{n}", [NH, TOK], t0 + j * TILE) for j, n in enumerate(("z", "e", "cum", "one")))
            lrow = at("lf_row", [P, ST + 1, NH], t0 + 4 * TILE)
            bias = at("lf_bias", [NH, 1], t0 + 4 * TILE + (ST + 1) * NH * 4)
            assert t0 + 4 * TILE + (ST + 1) * NH * 4 + 4 <= W + WBYTES - (ST + 1) * KVD * 4
            s_in, s_clear, s_hi, s_lo = sem("lf_loaded"), sem("lf_clear"), sem("lf_w_hi"), sem("lf_w_lo")
            s_mm, s_act, s_dve, s_t, s_out = sem("lf_product"), sem("lf_act"), sem("lf_dve"), sem("lf_turned"), sem("lf_stored")
            with phase() as block:
                @block.sync
                def _(sp):
                    sp.dma_start(wf[:, :, :], fox_w_f.rearrange("(k p) h -> p k h", p=P)).then_inc(s_in, 16)
                    sp.dma_start(bias[:, :], fox_b_f.rearrange("(h a) -> h a", a=1)).then_inc(s_in, 16)
                    sp.wait_ge(s_dve, 4)
                    sp.dma_start(logf_prompt[0].rearrange("(i p) h -> p i h", p=P), lrow[:, 0:ST, :]).then_inc(s_out, 16)
                    sp.dma_start(logf_sample[:, 0, :], lrow[0:NB, ST, :]).then_inc(s_out, 16)
                    sp.dma_start(ncum_dram, cum[:, 0:SEQ]).then_inc(s_out, 16)
                    sp.wait_ge(s_out, 48)

                @block.gpsimd
                def _(pool):
                    nc.gpsimd.memset(wf_hi[:, :, :].bitcast(F32), 0.0).then_inc(s_clear, 1)
                    nc.gpsimd.memset(wf_lo[:, :, :].bitcast(F32), 0.0).then_inc(s_clear, 1)
                    nc.gpsimd.memset(one[:, :], 1.0).then_inc(s_clear, 1)

                @block.scalar
                def _(act):
                    nc.scalar.preload_act_table_set(EXP_LN_SET)
                    act.wait_ge(s_in, 32)
                    act.wait_ge(s_clear, 3)
                    nc.scalar.activation(wf_hi[:, :, 0:NH], wf[:, :, :], ACT.Copy).then_inc(s_hi, 1)
                    act.wait_ge(s_mm, 1)
                    nc.scalar.activation(zb[:, :].rearrange("p (c n) -> p c n", c=CG), acc[0][0:NH, :, 0:NG],
                                         ACT.Identity, bias=bias[:, :]).then_inc(s_act, 1)
                    act.wait_ge(s_act, 1)
                    nc.scalar.activation(e[:, :], zb[:, :], ACT.Abs).then_inc(s_act, 1)
                    act.wait_ge(s_act, 2)
                    nc.scalar.activation(e[:, :], e[:, :], ACT.Exp, scale=-1.0).then_inc(s_act, 1)
                    act.wait_ge(s_act, 3)
                    nc.scalar.activation(e[:, :], e[:, :], ACT.Ln, bias=1.0).then_inc(s_act, 1)

                @block.tensor
                def _(pe):
                    pe.wait_ge(s_lo, 1)
                    split_product(acc[0], wf_hi, wf_lo, slice(0, P), h_hi, h_lo, KT).then_inc(s_mm, 1)
                    pe.wait_ge(s_dve, 1)
                    for i in range(ST + 1):
                        n = P if i < ST else NB
                        last = nc.tensor.transpose(bank[0][0:n, i * NH:(i + 1) * NH], zb[:, i * P:i * P + n],
                                                   ident[0:NH, 0:NH])
                    last.then_inc(s_t, 1)

                @block.vector
                def _(dve):
                    dve.wait_ge(s_hi, 1)
                    nc.vector.tensor_tensor(wf_lo[:, :, 0:NH], wf[:, :, :], wf_hi[:, :, 0:NH].bitcast(F32),
                                            ALU.subtract).then_inc(s_lo, 1)
                    dve.wait_ge(s_act, 4)
                    nc.vector.scalar_tensor_tensor(out=zb[:, :], in0=zb[:, :], scalar=0.0, in1=e[:, :],
                                                   op0=ALU.min, op1=ALU.subtract).then_inc(s_dve, 1)
                    dve.wait_ge(s_dve, 1)
                    nc.vector.tensor_tensor_scan(cum[:, 0:SEQ], one[:, 0:SEQ], zb[:, 0:SEQ], 0.0,
                                                 ALU.mult, ALU.add).then_inc(s_dve, 1)
                    dve.wait_ge(s_dve, 2)
                    nc.vector.tensor_scalar(cum[:, 0:SEQ], cum[:, 0:SEQ], -1.0, None, ALU.mult).then_inc(s_dve, 1)
                    dve.wait_ge(s_t, 1)
                    nc.vector.tensor_copy(lrow[:, 0:ST, :].rearrange("p i h -> p (i h)"), bank[0][:, 0:ST * NH])
                    nc.vector.tensor_copy(lrow[0:NB, ST, :], bank[0][0:NB, ST * NH:(ST + 1) * NH]).then_inc(s_dve, 1)
            return ((s_dve, 4),)

        TOKV = (ST + 1) * KVD * 4
        k_hi = at("k_hi", [P, 2, SEQ], W + TOKV, F32R)
        k_lo = at("k_lo", [P, 2, SEQ], W + TOKV + 2 * SEQ * 4, F32R)
        vcur = at("vcur", [P, ST, P], W + TOKV + 4 * SEQ * 4)
        qcur = [at(f"qcur{s}", [P, SEQ], W + TOKV + (5 + s) * SEQ * 4, F32R) for s in range(2)]
        WT = W + TOKV + 7 * SEQ * 4
        PAIRS = 2 * HG // 2
        STEPS = 2 * HG * ST
        TURNS = NKV // 2
        CUR = 2 * HG + 1
        COLS = NB * NPAGE * NH
        LOGF = W + WBYTES - 4 * COLS
        past_logf = at("past_logf", [P, NB, NPAGE, NH], LOGF)
        v_tiles = tokv[:, 0:ST, :].rearrange("p i (c n) -> p i c n", n=P)
        MULT1 = dict(scalar1=1.0, scalar2=None, op0=ALU.mult)

        def copy_keys_values(dve, t, s_part):
            def keys(gp):
                return kvT[half(gp), bass.ds(t, 1), 0:SEQ].rearrange("p a n -> p (a n)")
            for gp in range(2):
                for side in (gp, 1 - gp):
                    last = nc.vector.tensor_scalar(k_hi[half(side), gp, :], keys(gp), SCALE, None, ALU.mult)
                last.then_inc(s_part, 1)
            for gp in range(2):
                dve.wait_ge(s_part, CUR_PARTS * t + gp + 1)
                for side in (gp, 1 - gp):
                    nc.vector.scalar_tensor_tensor(out=k_lo[half(side), gp, :], in0=keys(gp), scalar=SCALE,
                                                   in1=k_hi[half(gp), gp, :].bitcast(F32), op0=ALU.mult, op1=ALU.subtract)
            return nc.vector.tensor_scalar(vcur[:, :, :], v_tiles[:, :, bass.ds(t, 1), :].rearrange("p i a n -> p i (a n)"),
                                           **MULT1)

        CUR_PARTS = 2 + 2 * HG

        def copy_queries(dve, t, hh, s_part):
            q = qT[half(hh), bass.ds(PAIRS * t + hh // 2, 1), 0:SEQ].rearrange("p a n -> p (a n)")
            nc.vector.tensor_scalar(qcur[hh % 2][half(hh), :], q, **MULT1).then_inc(s_part, 1)
            dve.wait_ge(s_part, CUR_PARTS * t + 3 + hh)
            return nc.vector.tensor_tensor(qcur[hh % 2][half(hh + 1), :], q, qcur[hh % 2][half(hh), :].bitcast(F32),
                                           ALU.subtract)

        def half(hh):
            return slice((hh % 2) * HALF, (hh % 2 + 1) * HALF)

        def pieces(a, b):
            while a < b:
                e = min(b, (a // 512 + 1) * 512)
                yield a, e
                a = e

        def stick_prompt():
            tiles = [B + j * SEQ * 4 for j in range(8)] + [WT + j * SEQ * 4 for j in range(4)] + \
                    [DD + (2 + j) * TILE for j in range(2)]
            ZS, ES = 7, 3
            zs = [at(f"st_z{j}", [P, SEQ], tiles[j]) for j in range(ZS)]
            es = [at(f"st_e{j}", [P, SEQ], tiles[ZS + j]) for j in range(ES)]
            sp_hi = [at(f"st_sp_hi{j}", [P, SEQ], tiles[10 + j], F32R) for j in range(2)]
            sp_lo = [at(f"st_sp_lo{j}", [P, SEQ], tiles[12 + j], F32R) for j in range(2)]
            AHEAD = 4
            tri_incl_r = at("tri_incl_r", [P, P], WT + 4 * SEQ * 4, F32R)
            tri_comp_r = at("tri_comp_r", [P, P], WT + 4 * SEQ * 4 + P * 4, F32R)
            key_mask = at("key_mask", [P, P], WT + 4 * SEQ * 4 + 2 * P * 4)
            assert WT + 4 * SEQ * 4 + 3 * P * 4 <= W + WBYTES
            z_ps = [flat(0, 2), flat(2, 4)]
            r_ps, o_ps = flat(4, 6), flat(6, 8)
            s_turn, s_part, s_cur = sem("st_turn"), sem("st_parts"), sem("st_copied")
            s_z, s_zc, s_e1, s_ln = sem("st_z_ready"), sem("st_z_copied"), sem("st_act"), sem("st_ln")
            s_sp, s_mask, s_r, s_arg = sem("st_sp"), sem("st_mask"), sem("st_r_ready"), sem("st_arg")
            s_hi, s_lo, s_comp = sem("st_sp_hi"), sem("st_sp_lo"), sem("st_r_completed")
            s_w, s_pv, s_o = sem("st_w"), sem("st_pv"), sem("st_o_copied")

            def key_block(n):
                return ST - 1 - n % ST

            def head(n):
                return n // ST

            def completed(t, n):
                return t * (STEPS - 2 * HG) + n + 1 - (n + 1) // ST

            def first_in_bank(b, col):
                return b == min(ST - 1, 4 * (col // 512) + 3)

            with phase() as block:
                @block.tensor
                def _(pe):
                    pe.sem_inc(s_turn, 1)

                    def scores(t, n):
                        b, hh = key_block(n), head(n)
                        if n % ST == 0:
                            pe.wait_ge(s_cur, CUR * t + 2 + hh)
                        if n >= 2:
                            pe.wait_ge(s_zc, t * STEPS + n - 1)
                        for c0, c1 in pieces(b * P, SEQ):
                            for keys in (k_hi, k_lo):
                                last = nc.tensor.matmul(z_ps[n % 2][:, c0:c1], keys[:, hh // HG, b * P:(b + 1) * P],
                                                        qcur[hh % 2][:, c0:c1], start=(keys is k_hi), stop=(keys is k_lo))
                        last.then_inc(s_z, 1)

                    def add_to_r(n, tri, first):
                        b = key_block(n)
                        for c0, c1 in pieces(b * P, SEQ):
                            for part in (sp_hi, sp_lo):
                                last = nc.tensor.matmul(r_ps[:, c0:c1], tri[:, :], part[n % 2][:, c0:c1],
                                                        start=first and part is sp_hi and first_in_bank(b, c0), stop=True,
                                                        skip_group_check=True)
                        return last

                    def values(t, n):
                        b, hh = key_block(n), head(n)
                        pe.wait_ge(s_w, t * STEPS + n + 1)
                        if n % ST == 0 and hh >= 1:
                            pe.wait_ge(s_o, 2 * HG * t + hh)
                        gp = hh // HG
                        for c0, c1 in pieces(b * P, SEQ):
                            last = nc.tensor.matmul(o_ps[0:HALF, c0:c1], vcur[:, b, gp * HALF:(gp + 1) * HALF],
                                                    zs[n % ZS][:, c0:c1], start=first_in_bank(b, c0), stop=True,
                                                    skip_group_check=True)
                        last.then_inc(s_pv, 1)

                    with pe.Fori(0, TURNS) as t:
                        for n in range(AHEAD + 1):
                            scores(t, n)
                        for n in range(STEPS):
                            pe.wait_ge(s_lo, t * STEPS + n + 1)
                            add_to_r(n, tri_incl_r, True).then_inc(s_r, 1)
                            if n + AHEAD + 1 < STEPS:
                                scores(t, n + AHEAD + 1)
                            if n >= 2:
                                values(t, n - 2)
                            pe.wait_ge(s_arg, t * STEPS + n + 1)
                            if key_block(n) > 0:
                                add_to_r(n, tri_comp_r, False).then_inc(s_comp, 1)
                        values(t, STEPS - 2)
                        values(t, STEPS - 1)
                        pe.wait_ge(s_pv, (t + 1) * STEPS)
                        pe.sem_inc(s_turn, 1)

                @block.vector
                def _(dve):
                    def copy_scores(t, n):
                        b = key_block(n)
                        dve.wait_ge(s_z, t * STEPS + n + 1)
                        if n >= ZS:
                            dve.wait_ge(s_pv, t * STEPS + n - ZS + 1)
                        own = nc.vector.tensor_tensor(zs[n % ZS][:, b * P:(b + 1) * P], z_ps[n % 2][:, b * P:(b + 1) * P],
                                                      key_mask[:, :], ALU.add)
                        if b < ST - 1:
                            own = nc.vector.tensor_copy(zs[n % ZS][:, (b + 1) * P:SEQ], z_ps[n % 2][:, (b + 1) * P:SEQ])
                        own.then_inc(s_zc, 1)
                        if n % ST == ST - 1 and head(n) + 2 < 2 * HG:
                            copy_queries(dve, t, head(n) + 2, s_part).then_inc(s_cur, 1)

                    def softplus(t, n):
                        b = key_block(n)
                        dve.wait_ge(s_ln, t * STEPS + n + 1)
                        e = es[n % ES][:, b * P:SEQ]
                        nc.vector.scalar_tensor_tensor(out=e, in0=zs[n % ZS][:, b * P:SEQ], scalar=0.0,
                                                       in1=e, op0=ALU.max, op1=ALU.add).then_inc(s_sp, 1)
                        dve.wait_ge(s_sp, t * STEPS + n + 1)
                        if n >= 2 and key_block(n - 2) > 0:
                            dve.wait_ge(s_comp, completed(t, n - 2))
                        elif n >= 2:
                            dve.wait_ge(s_r, t * STEPS + n - 1)
                        nc.vector.tensor_copy(sp_hi[n % 2][:, b * P:SEQ], e).then_inc(s_hi, 1)

                    def argument(t, n):
                        b = key_block(n)
                        dve.wait_ge(s_r, t * STEPS + n + 1)
                        nc.vector.tensor_tensor(zs[n % ZS][:, b * P:SEQ], zs[n % ZS][:, b * P:SEQ], r_ps[:, b * P:SEQ],
                                                ALU.subtract).then_inc(s_arg, 1)

                    def store_o(t, hh):
                        dve.wait_ge(s_pv, t * STEPS + (hh + 1) * ST)
                        nc.vector.tensor_scalar(oT[half(hh), bass.ds(PAIRS * t + hh // 2, 1), 0:SEQ].rearrange("p a n -> p (a n)"),
                                                o_ps[0:HALF, 0:SEQ], **MULT1).then_inc(s_o, 1)

                    for t_r, tri in ((tri_incl_r, tri_incl), (tri_comp_r, tri_comp)):
                        nc.vector.tensor_copy(t_r[:, :], tri[:, :])
                    nc.vector.tensor_scalar(key_mask[:, :], tri_comp[:, :], -1.0, -NEG, ALU.add, ALU.mult).then_inc(s_mask, 1)
                    dve.wait_ge(s_mask, 1)
                    with dve.Fori(0, TURNS) as t:
                        dve.wait_ge(s_turn, t + 1)
                        copy_keys_values(dve, t, s_part).then_inc(s_cur, 1)
                        copy_queries(dve, t, 0, s_part).then_inc(s_cur, 1)
                        copy_queries(dve, t, 1, s_part).then_inc(s_cur, 1)
                        for n in range(AHEAD):
                            copy_scores(t, n)
                        softplus(t, 0)
                        for n in range(STEPS):
                            if n + 1 < STEPS:
                                softplus(t, n + 1)
                            if n + AHEAD < STEPS:
                                copy_scores(t, n + AHEAD)
                            argument(t, n)
                            if n >= 2 and (n - 2) % ST == ST - 1:
                                store_o(t, head(n - 2))
                        store_o(t, 2 * HG - 1)

                @block.scalar
                def _(act):
                    nc.scalar.preload_act_table_set(EXP_LN_SET)

                    def log_part(t, n):
                        b = key_block(n)
                        e = es[n % ES][:, b * P:SEQ]
                        act.wait_ge(s_zc, t * STEPS + n + 1)
                        if n >= ES:
                            act.wait_ge(s_lo, t * STEPS + n - ES + 1)
                        nc.scalar.activation(e, zs[n % ZS][:, b * P:SEQ], ACT.Abs).then_inc(s_e1, 1)
                        act.wait_ge(s_e1, 2 * (t * STEPS + n) + 1)
                        nc.scalar.activation(e, e, ACT.Exp, scale=-1.0).then_inc(s_e1, 1)
                        act.wait_ge(s_e1, 2 * (t * STEPS + n) + 2)
                        nc.scalar.activation(e, e, ACT.Ln, bias=1.0).then_inc(s_ln, 1)

                    def weights(t, n):
                        b = key_block(n)
                        act.wait_ge(s_arg, t * STEPS + n + 1)
                        nc.scalar.activation(zs[n % ZS][:, b * P:SEQ], zs[n % ZS][:, b * P:SEQ], ACT.Exp).then_inc(s_w, 1)

                    with act.Fori(0, TURNS) as t:
                        log_part(t, 0)
                        log_part(t, 1)
                        for n in range(STEPS):
                            if n + 2 < STEPS:
                                log_part(t, n + 2)
                            if n >= 1:
                                weights(t, n - 1)
                        weights(t, STEPS - 1)

                @block.gpsimd
                def _(pool):
                    def low_part(t, n):
                        pool.wait_ge(s_hi, t * STEPS + n + 1)
                        cols = slice(key_block(n) * P, SEQ)
                        nc.gpsimd.tensor_tensor(sp_lo[n % 2][:, cols], es[n % ES][:, cols], sp_hi[n % 2][:, cols].bitcast(F32),
                                                ALU.subtract).then_inc(s_lo, 1)

                    with pool.Fori(0, TURNS) as t:
                        for n in range(STEPS):
                            low_part(t, n)

        def fox_prompt():
            tiles = [B + j * SEQ * 4 for j in range(8)]
            PT = 4
            pt = [at(f"fx_p{j}", [P, SEQ], (tiles[0], tiles[1], DD + 2 * TILE, DD + 3 * TILE)[j]) for j in range(PT)]
            tp = [at(f"fx_pT{j}", [P, SEQ], tiles[2 + j]) for j in range(2)]
            ncum = [at(f"fx_ncum{j}", [P, SEQ], tiles[4 + j]) for j in range(2)]
            opair = [at(f"fx_o{j}", [P, ST, P], tiles[6 + j]) for j in range(2)]
            stat = at("fx_stat", [P, 4, 4], WT)
            ident_r = at("ident_r", [P, P], WT + 64, F32R)
            causal_r = at("causal_r", [P, P], WT + 64 + P * 4, F32R)
            s_ps = [flat(0, 2), flat(2, 4)]
            t_ps = [psum[:, 4, :], psum[:, 5, :]]
            o_ps = [psum[:, 6, :], psum[:, 7, :]]
            s_turn, s_part, s_cur, s_seen = sem("fx_turn"), sem("fx_parts"), sem("fx_copied"), sem("fx_waits_seen")
            s_nc = [sem(f"fx_ncum_loaded{j}") for j in range(2)]
            s_s, s_max, s_nmax, s_p = sem("fx_scores"), sem("fx_max"), sem("fx_neg_max"), sem("fx_probs")
            s_t, s_ta, s_tv = sem("fx_turned"), sem("fx_turned_copied_act"), sem("fx_turned_copied_dve")
            s_pv, s_rc, s_o = sem("fx_pv"), sem("fx_recip"), sem("fx_o_copied")

            groups, of_step, of_pair = [], {}, {}

            def add_group(key, table, j, engine):
                table.setdefault(key, []).append(len(groups))
                groups.append((key, j, engine))

            def plan():
                for n in range(STEPS + 2):
                    if n < STEPS:
                        for j in range(0, n % ST + 1, 4):
                            add_group(n, of_step, j, "act" if len(groups) % 2 else "dve")
                    if n >= 2 and (n - 2) % (2 * ST) == 2 * ST - 1:
                        for j in range(0, ST, 4):
                            add_group((n - 2) // (2 * ST), of_pair, j, "dve")

            plan()
            GROUPS = len(groups)

            def copies(engine, upto):
                return sum(1 for g in groups[:upto + 1] if g[2] == engine)

            ALL = {e: copies(e, GROUPS - 1) for e in ("act", "dve")}

            logf = past_logf
            pages = at("fx_pages", [1, NB * NPAGE], LOGF - 4 * NB * NPAGE, I32)
            with phase() as block:
                @block.gpsimd
                def _(pool):
                    pool.dma_start(pages[:, :], row(page_table.rearrange("b n -> (b n)"))).then_inc(s_pool_load, 16)
                    pool.wait_ge(s_pool_load, 16)
                    with pool.Fori(0, NB * NPAGE) as at_:
                        pid = pool.value_load(pages[0:1, bass.ds(at_, 1)], min_val=0, max_val=POOL - 1)
                        pool.dma_start(logf[:, :, :, :].rearrange("p b n h -> p (b n) h")[:, bass.ds(at_, 1), :]
                                       .rearrange("p a h -> p (a h)"),
                                       cache_logf[bass.ds(pid, 1)].rearrange("a t h -> t (a h)")).then_inc(s_pool_load, 16)
                    pool.wait_ge(s_pool_load, 16 * (NB * NPAGE + 1))

                @block.sync
                def _(sp):
                    with sp.Fori(0, TURNS) as t:
                        for hh in range(2 * HG):
                            if hh < 2:
                                sp.wait_ge(s_turn, t + 1)
                            else:
                                sp.wait_ge(s_max, t * STEPS + (hh - 1) * ST)
                            sp.dma_start(ncum[hh % 2][:, :], ncum_dram[bass.ds(2 * HG * t + hh, 1), :].partition_broadcast(P))\
                                .then_inc(s_nc[hh % 2], 16)

                @block.tensor
                def _(pe):
                    pe.sem_inc(s_turn, 1)

                    def scores(t, n):
                        i, hh = n % ST, n // ST
                        if n % ST == 0:
                            pe.wait_ge(s_cur, CUR * t + 2 + hh)
                        if n >= 2:
                            pe.wait_ge(s_max, t * STEPS + n - 1)
                        q = qcur[hh % 2][:, i * P:(i + 1) * P]
                        for c0, c1 in pieces(0, (i + 1) * P):
                            for keys in (k_hi, k_lo):
                                nc.tensor.matmul(s_ps[n % 2][:, c0:c1], q, keys[:, hh // HG, c0:c1],
                                                 start=(keys is k_hi), stop=(keys is k_lo))
                        nc.tensor.matmul(s_ps[n % 2][:, i * P:(i + 1) * P], ident_r[:, :], causal_r[:, :], start=False, stop=True,
                                         skip_group_check=True).then_inc(s_s, 1)

                    def bank_free(t, g):
                        if g >= 2:
                            e = groups[g - 2][2]
                            pe.wait_ge(s_ta if e == "act" else s_tv, t * ALL[e] + copies(e, g - 2))

                    def turn_probs(t, n):
                        i = n % ST
                        pe.wait_ge(s_p, t * STEPS + n + 1)
                        for g in of_step[n]:
                            bank_free(t, g)
                            j0 = groups[g][1]
                            for j in range(j0, min(j0 + 4, i + 1)):
                                last = nc.tensor.transpose(t_ps[g % 2][:, (j - j0) * P:(j - j0 + 1) * P],
                                                           pt[n % PT][:, j * P:(j + 1) * P], ident[:, :])
                            last.then_inc(s_t, 1)

                    def turn_outputs(t, pr):
                        pe.wait_ge(s_o, t * STEPS + (pr + 1) * 2 * ST)
                        for g in of_pair[pr]:
                            bank_free(t, g)
                            j0 = groups[g][1]
                            for j in range(j0, min(j0 + 4, ST)):
                                last = nc.tensor.transpose(t_ps[g % 2][:, (j - j0) * P:(j - j0 + 1) * P],
                                                           opair[pr % 2][:, j, :], ident[:, :])
                            last.then_inc(s_t, 1)

                    def values(t, n):
                        i, hh = n % ST, n // ST
                        gs = of_step[n]
                        for e, s in (("act", s_ta), ("dve", s_tv)):
                            if any(groups[g][2] == e for g in gs):
                                pe.wait_ge(s, t * ALL[e] + copies(e, gs[-1]))
                        if n >= 2:
                            pe.wait_ge(s_o, t * STEPS + n - 1)
                        gp = hh // HG
                        for j in range(i + 1):
                            last = nc.tensor.matmul(o_ps[n % 2][:, 0:HALF], tp[n % 2][:, j * P:(j + 1) * P],
                                                    vcur[:, j, gp * HALF:(gp + 1) * HALF], start=(j == 0), stop=(j == i))
                        last.then_inc(s_pv, 1)

                    with pe.Fori(0, TURNS) as t:
                        for n in range(3):
                            scores(t, n)
                        for n in range(STEPS + 2):
                            if n < STEPS:
                                turn_probs(t, n)
                            if 1 <= n <= STEPS:
                                values(t, n - 1)
                            if n >= 2 and (n - 2) % (2 * ST) == 2 * ST - 1:
                                turn_outputs(t, (n - 2) // (2 * ST))
                            if n + 3 < STEPS:
                                scores(t, n + 3)
                        pe.wait_ge(s_tv, (t + 1) * ALL["dve"])
                        pe.sem_inc(s_turn, 1)

                @block.vector
                def _(dve):
                    def add_decay(t, n):
                        i, hh = n % ST, n // ST
                        L = (i + 1) * P
                        if i == 0:
                            dve.wait_ge(s_nc[hh % 2], 16 * (HG * t + hh // 2 + 1))
                        if n >= PT:
                            dve.wait_ge(s_t, t * GROUPS + of_step[n - PT][-1] + 1)
                        dve.wait_ge(s_s, t * STEPS + n + 1)
                        dve.sem_inc(s_seen, 1)
                        st = stat[:, n % 4, :]
                        nc.vector.tensor_tensor_reduce(pt[n % PT][:, 0:L], s_ps[n % 2][:, 0:L], ncum[hh % 2][:, 0:L], 1.0, -3.0e38,
                                                       ALU.add, ALU.max, st[:, 0:1]).then_inc(s_max, 1)
                        dve.wait_ge(s_max, t * STEPS + n + 1)
                        nc.vector.tensor_scalar(st[:, 1:2], st[:, 0:1], -1.0, None, ALU.mult).then_inc(s_nmax, 1)

                    def copy_step(t, n):
                        for g in of_step[n]:
                            if groups[g][2] == "dve":
                                dve.wait_ge(s_t, t * GROUPS + g + 1)
                                j0 = groups[g][1]
                                w = (min(j0 + 4, n % ST + 1) - j0) * P
                                if n >= 2:
                                    dve.wait_ge(s_pv, t * STEPS + n - 1)
                                nc.vector.tensor_copy(tp[n % 2][:, j0 * P:j0 * P + w], t_ps[g % 2][:, 0:w]).then_inc(s_tv, 1)

                    def copy_pair(t, pr):
                        for g in of_pair[pr]:
                            dve.wait_ge(s_t, t * GROUPS + g + 1)
                            j0 = groups[g][1]
                            w = (min(j0 + 4, ST) - j0) * P
                            nc.vector.tensor_scalar(oT[:, bass.ds(PAIRS * t + pr, 1), j0 * P:j0 * P + w].rearrange("p a n -> p (a n)"),
                                                    t_ps[g % 2][:, 0:w], **MULT1).then_inc(s_tv, 1)

                    def normalise(t, n):
                        i, hh = n % ST, n // ST
                        st = stat[:, n % 4, :]
                        dve.wait_ge(s_p, t * STEPS + n + 1)
                        nc.vector.reciprocal(st[:, 3:4], st[:, 2:3]).then_inc(s_rc, 1)
                        if hh >= 4 and n % (2 * ST) == 0:
                            dve.wait_ge(s_t, t * GROUPS + of_pair[hh // 2 - 2][-1] + 1)
                        dve.wait_ge(s_rc, t * STEPS + n + 1)
                        dve.wait_ge(s_pv, t * STEPS + n + 1)
                        nc.vector.tensor_scalar(opair[hh // 2 % 2][:, i, half(hh)], o_ps[n % 2][:, 0:HALF], st[:, 3:4], None,
                                                ALU.mult).then_inc(s_o, 1)

                    nc.vector.tensor_copy(ident_r[:, :], ident[:, :])
                    nc.vector.tensor_copy(causal_r[:, :], causal[:, :])
                    with dve.Fori(0, TURNS) as t:
                        dve.wait_ge(s_turn, t + 1)
                        copy_keys_values(dve, t, s_part).then_inc(s_cur, 1)
                        copy_queries(dve, t, 0, s_part).then_inc(s_cur, 1)
                        copy_queries(dve, t, 1, s_part).then_inc(s_cur, 1)
                        add_decay(t, 0)
                        add_decay(t, 1)
                        for n in range(STEPS + 2):
                            if n < STEPS:
                                copy_step(t, n)
                            if n + 2 < STEPS:
                                add_decay(t, n + 2)
                                if (n + 2) % ST == ST - 1 and (n + 2) // ST + 2 < 2 * HG:
                                    copy_queries(dve, t, (n + 2) // ST + 2, s_part).then_inc(s_cur, 1)
                            if 1 <= n <= STEPS:
                                normalise(t, n - 1)
                            if n >= 2 and (n - 2) % (2 * ST) == 2 * ST - 1:
                                copy_pair(t, (n - 2) // (2 * ST))

                @block.scalar
                def _(act):
                    def probs(t, n):
                        L = (n % ST + 1) * P
                        st = stat[:, n % 4, :]
                        act.wait_ge(s_nmax, t * STEPS + n + 1)
                        nc.scalar.activation(pt[n % PT][:, 0:L], pt[n % PT][:, 0:L], ACT.Exp, bias=st[:, 1:2],
                                             accum_out=st[:, 2:3]).then_inc(s_p, 1)

                    def copy_step(t, n):
                        for g in of_step[n]:
                            if groups[g][2] == "act":
                                j0 = groups[g][1]
                                w = (min(j0 + 4, n % ST + 1) - j0) * P
                                act.wait_ge(s_t, t * GROUPS + g + 1)
                                if n >= 2:
                                    act.wait_ge(s_pv, t * STEPS + n - 1)
                                nc.scalar.activation(tp[n % 2][:, j0 * P:j0 * P + w], t_ps[g % 2][:, 0:w], ACT.Copy)\
                                    .then_inc(s_ta, 1)

                    with act.Fori(0, TURNS) as t:
                        probs(t, 0)
                        probs(t, 1)
                        for n in range(STEPS):
                            copy_step(t, n)
                            if n + 2 < STEPS:
                                probs(t, n + 2)

        HALVES = 2
        HH = NH // HALVES
        QUADS = NPAGE // 4
        assert NPAGE % 4 == 0 and QUADS % 2 == 0 and NB % 2 == 0 and COLS <= 2048 and NB * NH == P

        def decode(l):
            fox = l == 1
            PG = NPAGE + 1 if fox else NPAGE
            BUFS = 4
            off = [W]

            def tile(name, shape, dt=F32):
                n = 4
                for x in shape[1:]:
                    n *= x
                t = at(f"dc_{name}{l}", shape, off[0], dt)
                off[0] += n + (-n % 32)
                assert off[0] <= LOGF
                return t

            page = [tile(f"page{j}", [P, 4, KVD]) for j in range(BUFS)]
            turned_hi = [tile(f"turned_hi{j}", [P, HALVES, 4 * P], F32R) for j in range(2)]
            score = tile("score", [P, NB, PG, NH])
            part = tile("part", [P, NB, PG, NH])
            turned_lo = [at(f"dc_turned_lo{j}_{l}", [P, HALVES, 4 * P], off[0] - 4 * NB * PG * NH + j * HALVES * 16 * P, F32R)
                         for j in range(2)]
            assert HALVES * 8 * P <= NB * NPAGE * NH
            odec = tile("odec", [P, HALVES, NB, HH])
            small = tile("small", [P, 4, NB * NH])
            pages = tile("pages", [1, NB * NPAGE], I32)
            suffix = at(f"dc_suffix{l}", [P, NB, NPAGE, NH], B)
            logf = past_logf
            boff = [B + 4 * COLS + 4 * NB * KVD + 4 * NB * NH]

            def btile(name, shape, dt=F32):
                n = 4
                for x in shape[1:]:
                    n *= x
                t = at(f"dc_{name}{l}", shape, boff[0], dt)
                boff[0] += n
                assert boff[0] <= B + KTILES
                return t

            qall = btile("qall", [P, HALVES, NB, NH])
            qall_hi, qall_lo = (btile(f"qall_{n}", [P, HALVES, NB, NH], F32R) for n in ("hi", "lo"))
            qseq_hi, qseq_lo = ([btile(f"qseq_{n}{u}_", [P, HALVES, NB, NH], F32R) for u in range(2)] for n in ("hi", "lo"))
            zero = btile("zero", [P, P])
            srow = btile("srow", [P, QUADS, 4 * P])
            vtail = at(f"dc_vtail{l}", [1, NB, KVD], B + 4 * COLS)
            lnew = at(f"dc_lnew{l}", [P, NB * NH], B + 4 * COLS + 4 * NB * KVD)
            t_ps = [flat(0, 2), flat(2, 4)]

            def queries_of(h):
                g = h // HG
                return g // 2, g % 2, (g % 2) * HG + h % HG

            def page_loop(engine, body):
                with engine.Fori(0, NB // 2) as bb:
                    for u in range(2):
                        body(bb, u)

            def page_semaphores(name):
                even = [sem(f"{name}_buffer{j}") for j in (0, 2)]
                return [even[0], s_pool_page[0], even[1], s_pool_page[1]]

            def pages_loaded(stage, bb, n):
                before = 64 * (2 * l + stage) * (NB * NPAGE // (4 * BUFS)) if n % 2 else 0
                return before + 64 * (TURN // BUFS * bb + n // BUFS + 1)

            s_pt, s_q0, s_q = sem(f"dk_table_{l}"), sem(f"dk_q_clear_{l}"), sem(f"dk_q_{l}")
            s_page = page_semaphores(f"dk_page_{l}")
            s_turned, s_hi, s_lo, s_sc = (sem(f"dk_{n}_{l}") for n in ("turned", "turned_hi", "turned_lo", "scores"))
            s_new, s_neg, s_free = (sem(f"dk_{n}_{l}") for n in ("new_scores", "tail_clear", "new_scores_copied"))
            s_clear, s_qseq = sem(f"dk_q_seq_clear_{l}"), sem(f"dk_q_seq_{l}")
            s_ra, s_rd, s_back = sem(f"dk_rows_act_{l}"), sem(f"dk_rows_dve_{l}"), sem(f"dk_turned_back_{l}")
            TURN = 2 * QUADS

            def load_pages(engine, bb, u, odd, cache, sems, free):
                for qd in range(odd, QUADS, 2):
                    n = u * QUADS + qd
                    engine.wait_ge(free, TURN * bb + n + 1)
                    for j in range(4):
                        at_ = (2 * bb + u) * NPAGE + 4 * qd + j
                        pid = engine.value_load(pages[0:1, bass.ds(at_, 1)], min_val=0, max_val=POOL - 1)
                        engine.dma_start(page[n % BUFS][:, j, :],
                                         cache[l, bass.ds(pid, 1)].rearrange("a t g d -> t (a g d)")).then_inc(sems[n % BUFS], 16)

            with phase() as block:
                @block.sync
                def _(sp):
                    sp.dma_start(pages[:, :], row(page_table.rearrange("b n -> (b n)"))).then_inc(s_pt, 16)
                    sp.wait_ge(s_pt, 16)
                    page_loop(sp, lambda bb, u: load_pages(sp, bb, u, 0, cache_k, s_page, s_turned))

                @block.gpsimd
                def _(pool):
                    pool.wait_ge(s_pt, 16)
                    if fox:
                        pool.dma_start(lnew[:, :], row(logf_sample.rearrange("b a h -> (b a h)")).partition_broadcast(P))\
                            .then_inc(s_pool_load, 16)
                        pool.dma_start(vtail[:, :, :].rearrange("p b n -> p (b n)"),
                                       row(v_sample[l].rearrange("b a g d -> (b a g d)"))).then_inc(s_pool_load, 16)
                    page_loop(pool, lambda bb, u: load_pages(pool, bb, u, 1, cache_k, s_page, s_turned))
                    if fox:
                        pool.wait_ge(s_pool_load, 16 * (NB * NPAGE + 3))

                @block.tensor
                def _(pe):
                    pe.sem_inc(s_turned, BUFS)
                    pe.wait_ge(s_q, 3)
                    if fox:
                        for b in range(NB):
                            for hf in range(HALVES):
                                heads = slice(hf * HH, (hf + 1) * HH)
                                last = nc.tensor.matmul(bank[0][0:1, (b * HALVES + hf) * HH:(b * HALVES + hf + 1) * HH],
                                                        kvT[:, hf, SEQ + b:SEQ + b + 1], qall[:, hf, b, heads], start=True, stop=True)
                        last.then_inc(s_new, 1)
                        pe.wait_ge(s_free, 1)
                    for c in range(4 * QUADS):
                        nc.tensor.matmul(psum[:, 4 + c // 4, c % 4 * P:(c % 4 + 1) * P], zero[:, :], ones[:, :], start=True, stop=True)

                    def turn(bb, n):
                        pe.wait_ge(s_page[n % BUFS], pages_loaded(0, bb, n))
                        if n >= 2:
                            pe.wait_ge(s_lo, TURN * bb + n - 1)
                        for j in range(4):
                            for hf in range(HALVES):
                                last = nc.tensor.transpose(t_ps[n % 2][:, (hf * 4 + j) * P:(hf * 4 + j + 1) * P],
                                                           page[n % BUFS][:, j, hf * P:(hf + 1) * P], ident[:, :])
                        last.then_inc(s_turned, 1)

                    def scores(bb, n):
                        u, qd = n // QUADS, n % QUADS
                        pe.wait_ge(s_lo, TURN * bb + n + 1)
                        if qd == 0:
                            pe.wait_ge(s_qseq, 2 * bb + u + 1)
                        for hf in range(HALVES):
                            for q, k in ((qseq_hi, turned_hi), (qseq_hi, turned_lo), (qseq_lo, turned_hi)):
                                last = nc.tensor.matmul(psum[:, 4 + qd, 0:4 * P], q[u][:, hf, :, :].rearrange("p b h -> p (b h)"),
                                                        k[n % 2][:, hf, :], start=False, stop=True, skip_group_check=True)
                        last.then_inc(s_sc, 1)

                    with pe.Fori(0, NB // 2) as bb:
                        turn(bb, 0)
                        for n in range(TURN):
                            if n + 1 < TURN:
                                turn(bb, n + 1)
                            scores(bb, n)
                    pe.wait_ge(s_ra, 1)
                    pe.wait_ge(s_rd, 1)
                    for n in range(NPAGE):
                        last = nc.tensor.transpose(psum[:, n // 4, n % 4 * P:(n % 4 + 1) * P],
                                                   srow[:, n // 4, n % 4 * P:(n % 4 + 1) * P], ident[:, :])
                    last.then_inc(s_back, 1)

                HQ = QUADS // 2

                def turned_back(q0):
                    src = psum[:, q0:q0 + HQ, :].rearrange("p q n -> p (q n)").rearrange("p (n b h) -> p b n h", b=NB, h=NH)
                    return score[:, :, 4 * q0:4 * (q0 + HQ), :], src

                @block.scalar
                def _(act):
                    with act.Fori(0, NB // 2) as bb:
                        for n in range(TURN):
                            act.wait_ge(s_turned, TURN * bb + n + 1 + BUFS)
                            if n >= 2:
                                act.wait_ge(s_sc, TURN * bb + n - 1)
                            nc.scalar.activation(turned_hi[n % 2][:, :, :].rearrange("p f n -> p (f n)"), t_ps[n % 2][:, :],
                                                 ACT.Copy).then_inc(s_hi, 1)
                    act.wait_ge(s_sc, NB * QUADS)
                    nc.scalar.activation(srow[:, HQ:QUADS, :], psum[:, 4 + HQ:4 + QUADS, :], ACT.Copy).then_inc(s_ra, 1)
                    act.wait_ge(s_back, 1)
                    dst, src = turned_back(HQ)
                    nc.scalar.activation(dst, src, ACT.Copy)

                @block.vector
                def _(dve):
                    nc.vector.memset(qall[:, :, :, :], 0.0).then_inc(s_q0, 1)
                    nc.vector.memset(zero[:, :], 0.0)
                    if fox:
                        nc.vector.memset(score[:, :, NPAGE, :], NEG).then_inc(s_neg, 1)
                    dve.wait_ge(s_q0, 1)
                    for h in range(NH):
                        hf, side, c = queries_of(h)
                        last = nc.vector.tensor_scalar(qall[side * HALF:(side + 1) * HALF, hf, :, hf * HH + c],
                                                       qT[(h % 2) * HALF:(h % 2 + 1) * HALF, h // 2, SEQ:TOK],
                                                       SCALE, None, ALU.mult)
                    last.then_inc(s_q, 1)
                    dve.wait_ge(s_q, 1)
                    nc.vector.tensor_copy(qall_hi[:, :, :, :], qall[:, :, :, :]).then_inc(s_q, 1)
                    dve.wait_ge(s_q, 2)
                    nc.vector.tensor_tensor(qall_lo[:, :, :, :], qall[:, :, :, :], qall_hi[:, :, :, :].bitcast(F32),
                                            ALU.subtract).then_inc(s_q, 1)
                    dve.wait_ge(s_q, 3)
                    if fox:
                        dve.wait_ge(s_new, 1)
                        dve.wait_ge(s_neg, 1)
                        nc.vector.tensor_copy(score[0:1, :, NPAGE, :], bank[0][0:1, 0:NB * NH].rearrange("p (b h) -> p b h", b=NB))\
                            .then_inc(s_free, 1)

                    def queries_of_sequence(b, u):
                        nc.vector.memset(qseq_hi[u][:, :, :, :].bitcast(F32), 0.0)
                        nc.vector.memset(qseq_lo[u][:, :, :, :].bitcast(F32), 0.0).then_inc(s_clear, 1)
                        dve.wait_ge(s_clear, b + 1)
                        for seq, every in ((qseq_hi, qall_hi), (qseq_lo, qall_lo)):
                            last = nc.vector.tensor_scalar(seq[u][:, :, bass.ds(b, 1), :], every[:, :, bass.ds(b, 1), :].bitcast(F32),
                                                           **MULT1)
                        last.then_inc(s_qseq, 1)

                    def body(bb, last):
                        for n in range(TURN):
                            dve.wait_ge(s_hi, TURN * bb + n + 1)
                            nc.vector.tensor_tensor(turned_lo[n % 2][:, :, :].rearrange("p f n -> p (f n)"), t_ps[n % 2][:, :],
                                                    turned_hi[n % 2][:, :, :].rearrange("p f n -> p (f n)").bitcast(F32),
                                                    ALU.subtract).then_inc(s_lo, 1)
                            if n == 1:
                                queries_of_sequence(2 * bb + 1, 1)
                            if n == QUADS + 1 and not last:
                                queries_of_sequence(2 * bb + 2, 0)

                    queries_of_sequence(0, 0)
                    with dve.Fori(0, NB // 2 - 1) as bb:
                        body(bb, False)
                    body(NB // 2 - 1, True)
                    dve.wait_ge(s_sc, NB * QUADS)
                    nc.vector.tensor_copy(srow[:, 0:HQ, :], psum[:, 4:4 + HQ, :]).then_inc(s_rd, 1)
                    dve.wait_ge(s_back, 1)
                    dst, src = turned_back(0)
                    nc.vector.tensor_copy(dst, src)

            with together():
                s_a, s_v, s_p = sem(f"dw_act_{l}"), sem(f"dw_dve_{l}"), sem(f"dw_pe_{l}")
                s_page_v = page_semaphores(f"dv_page_{l}")
                s_seen = sem(f"dv_waits_seen_{l}")
                s_used, s_wc, s_rows, s_turned_o, s_oc, s_tail = (sem(f"dv_{n}_{l}") for n in (
                    "used", "weights_copied", "rows_copied", "turned", "copied", "tail"))
                wcur = [at(f"dv_wcur{u}_{l}", [P, NPAGE, NH], W + (BUFS * 4 * KVD + u * NPAGE * NH) * 4) for u in range(2)]
                orow = [at(f"dv_orow{u}_{l}", [NH, KVD], W + (BUFS * 4 * KVD + 2 * NPAGE * NH + u * KVD) * 4) for u in range(2)]
                assert 2 * (NPAGE * NH + KVD) <= 8 * HALVES * P
                c_ps, tot_ps = flat(0, 4), flat(4, 8)
                past = score[:, :, 0:NPAGE, :]
                summand = logf if fox else part

                def bnh(ap):
                    return ap[:, 0:COLS].rearrange("p (b n h) -> p b n h", b=NB, n=NPAGE)

                with phase() as block:
                    @block.scalar
                    def _(act):
                        nc.scalar.preload_act_table_set(EXP_LN_SET)
                        if not fox:
                            nc.scalar.activation(part[:, :, :, :], past, ACT.Abs).then_inc(s_a, 1)
                            act.wait_ge(s_a, 1)
                            nc.scalar.activation(part[:, :, :, :], part[:, :, :, :], ACT.Exp, scale=-1.0).then_inc(s_a, 1)
                            act.wait_ge(s_a, 2)
                            nc.scalar.activation(part[:, :, :, :], part[:, :, :, :], ACT.Ln, bias=1.0).then_inc(s_a, 1)
                        act.wait_ge(s_v, NPAGE + (7 if fox else 3))
                        nc.scalar.activation(score[:, :, :, :], score[:, :, :, :], ACT.Exp).then_inc(s_a, 1)

                    @block.tensor
                    def _(pe):
                        pe.sem_inc(s_used, BUFS)
                        if not fox:
                            pe.wait_ge(s_v, 1)
                        flat_in = summand[:, :, :, :].rearrange("p b n h -> p (b n h)")
                        for tri, out in ((tri_strict if fox else tri_incl, c_ps), (ones, tot_ps)):
                            for c0, c1 in pieces(0, COLS):
                                last = nc.tensor.matmul(out[:, c0:c1], tri[:, :], flat_in[:, c0:c1], start=True, stop=True)
                        last.then_inc(s_p, 1)
                        if fox:
                            pe.wait_ge(s_v, NPAGE + 3)
                            nc.tensor.transpose(psum[:, 0, 0:P], small[:, 0, :], ident[:, :]).then_inc(s_p, 1)
                            pe.wait_ge(s_v, NPAGE + 5)
                            nc.tensor.matmul(psum[:, 1, 0:P], ones[:, :], small[:, 2, :], start=True, stop=True).then_inc(s_p, 1)
                            pe.wait_ge(s_v, NPAGE + 8)
                            nc.tensor.matmul(psum[:, 2, 0:P], ones[:, :], small[:, 0, :], start=True, stop=True).then_inc(s_p, 1)

                    @block.vector
                    def _(dve):
                        done = [0]

                        def step(ins):
                            done[0] += 1
                            ins.then_inc(s_v, 1)
                            dve.wait_ge(s_v, done[0])

                        if not fox:
                            dve.wait_ge(s_a, 3)
                            step(nc.vector.scalar_tensor_tensor(out=part[:, :, :, :], in0=past, scalar=0.0, in1=part[:, :, :, :],
                                                                op0=ALU.max, op1=ALU.add))
                            step(nc.vector.memset(suffix[:, :, NPAGE - 1, :], 0.0))
                        else:
                            step(nc.vector.tensor_copy(suffix[:, :, NPAGE - 1, :], lnew[:, :].rearrange("p (b h) -> p b h", b=NB)))
                        dve.wait_ge(s_p, 1)
                        total = bnh(tot_ps)
                        for n in range(NPAGE - 2, -1, -1):
                            step(nc.vector.tensor_tensor(suffix[:, :, n, :], total[:, :, n + 1, :], suffix[:, :, n + 1, :], ALU.add))
                        op = ALU.add if fox else ALU.subtract
                        step(nc.vector.tensor_tensor(past, past, suffix[:, :, :, :], op))
                        flat_c = bnh(c_ps)
                        if not fox:
                            step(nc.vector.tensor_tensor(past, past, flat_c, ALU.subtract))
                            assert done[0] == NPAGE + 3
                            return
                        step(nc.vector.tensor_tensor(past, past, flat_c, ALU.add))
                        by_head = score[:, :, :, :].rearrange("p b n h -> p b h n")
                        step(nc.vector.tensor_reduce(small[:, 0, :].rearrange("p (b h) -> p b h", b=NB), by_head, AX.X, ALU.max))
                        dve.wait_ge(s_p, 2)
                        assert done[0] == NPAGE + 3, done
                        step(nc.vector.tensor_reduce(small[:, 1, 0:1], psum[:, 0, 0:P], AX.X, ALU.max))
                        step(nc.vector.tensor_scalar(small[:, 2, :], ident[:, :], small[:, 1, 0:1], None, ALU.mult))
                        dve.wait_ge(s_p, 3)
                        step(nc.vector.tensor_copy(small[:, 3, :], psum[:, 1, 0:P]))
                        top = small[:, 3, :].rearrange("p (b a h) -> p b a h", b=NB, a=1)
                        step(nc.vector.tensor_tensor(score[:, :, :, :], score[:, :, :, :], top.broadcast_to([P, NB, PG, NH]),
                                                     ALU.subtract))
                        assert done[0] == NPAGE + 7
                        dve.wait_ge(s_a, 1)
                        step(nc.vector.tensor_reduce(small[:, 0, :].rearrange("p (b h) -> p b h", b=NB), by_head, AX.X, ALU.add))
                        dve.wait_ge(s_p, 4)
                        step(nc.vector.reciprocal(small[:, 1, :], psum[:, 2, 0:P]))

                s_od = sem(f"dv_done_{l}")
                with phase() as block:
                    @block.sync
                    def _(sp):
                        page_loop(sp, lambda bb, u: load_pages(sp, bb, u, 0, cache_v, s_page_v, s_used))

                    @block.gpsimd
                    def _(pool):
                        page_loop(pool, lambda bb, u: load_pages(pool, bb, u, 1, cache_v, s_page_v, s_used))

                    @block.tensor
                    def _(pe):
                        pe.wait_ge(s_a, 1 if fox else 4)
                        if fox:
                            for b in range(NB):
                                for hf in range(HALVES):
                                    c = (b * HALVES + hf) * HH
                                    last = nc.tensor.matmul(psum[:, 0, c:c + HH], vtail[0:1, b, hf * P:(hf + 1) * P],
                                                            score[0:1, b, NPAGE, hf * HH:(hf + 1) * HH], start=True, stop=True)
                            last.then_inc(s_tail, 1)

                        def turn_output(bb, u):
                            pe.wait_ge(s_rows, 2 * bb + u + 3)
                            pe.wait_ge(s_oc, 2 * bb + u + 1)
                            pe.sem_inc(s_seen, 1)
                            for hf in range(HALVES):
                                last = nc.tensor.transpose(psum[:, 6 + u, hf * NH:(hf + 1) * NH], orow[u][:, hf * P:(hf + 1) * P],
                                                           ident[0:NH, 0:NH])
                            last.then_inc(s_turned_o, 1)

                        with pe.Fori(0, NB // 2) as bb:
                            for n in range(TURN):
                                u, qd = n // QUADS, n % QUADS
                                pe.wait_ge(s_page_v[n % BUFS], pages_loaded(1, bb, n))
                                if qd == 0:
                                    pe.wait_ge(s_wc, 2 * bb + u + 1)
                                    pe.wait_ge(s_rows, 2 * bb + u + 1)
                                for j in range(4):
                                    last = nc.tensor.matmul(psum[0:NH, 4 + u, 0:KVD], wcur[u][:, 4 * qd + j, :],
                                                            page[n % BUFS][:, j, :], start=(qd == 0 and j == 0),
                                                            stop=(qd == QUADS - 1 and j == 3))
                                last.then_inc(s_used, 1)
                                if n == QUADS:
                                    turn_output(bb, 0)
                            turn_output(bb, 1)

                    @block.vector
                    def _(dve):
                        dve.wait_ge(s_a, 1 if fox else 4)
                        dve.sem_inc(s_rows, 2)
                        dve.sem_inc(s_oc, 2)

                        def copy_weights(b, u):
                            nc.vector.tensor_scalar(wcur[u][:, :, :], score[:, bass.ds(b, 1), 0:NPAGE, :]
                                                    .rearrange("p a n h -> p (a n) h"), **MULT1).then_inc(s_wc, 1)

                        def body(bb, last):
                            for u in range(2):
                                dve.wait_ge(s_used, TURN * bb + (u + 1) * QUADS + BUFS)
                                nc.vector.tensor_scalar(orow[u][:, :], psum[0:NH, 4 + u, 0:KVD], **MULT1).then_inc(s_rows, 1)
                                if not last:
                                    copy_weights(2 * bb + u + 2, u)
                                dve.wait_ge(s_turned_o, 2 * bb + u + 1)
                                own = psum[:, 6 + u, 0:HALVES * (NH + HH)].rearrange("p (f c) -> p f c", f=HALVES)[:, :, 0:HH]
                                nc.vector.tensor_scalar(odec[:, :, bass.ds(2 * bb + u, 1), :].rearrange("p f a h -> p f (a h)"),
                                                        own, **MULT1).then_inc(s_oc, 1)

                        copy_weights(0, 0)
                        copy_weights(1, 1)
                        with dve.Fori(0, NB // 2 - 1) as bb:
                            body(bb, False)
                        body(NB // 2 - 1, True)
                        dve.wait_ge(s_oc, NB + 2)
                        if fox:
                            dve.wait_ge(s_tail, 1)
                            nc.vector.tensor_tensor(odec[:, :, :, :], psum[:, 0, 0:NB * NH].rearrange("p (b f h) -> p f b h", b=NB, f=HALVES),
                                                    odec[:, :, :, :], ALU.add).then_inc(s_od, 1)
                            dve.wait_ge(s_od, 1)
                            rden = small[:, 1, :].rearrange("p (b f h) -> p f b h", b=NB, f=HALVES)
                            nc.vector.tensor_tensor(odec[:, :, :, :], odec[:, :, :, :], rden, ALU.mult).then_inc(s_od, 1)
                            dve.wait_ge(s_od, 2)
                        for h in range(NH):
                            hf, side, c = queries_of(h)
                            nc.vector.tensor_copy(oT[(h % 2) * HALF:(h % 2 + 1) * HALF, h // 2, SEQ:TOK],
                                                  odec[side * HALF:(side + 1) * HALF, hf, :, c])

        setup()
        for l in range(DEPTH):
            with together():
                project_qkv(l, norm(f"mix{l}", l))
            with together():
                kv_rows(l, log_forget() if l == 1 else ())
            if l == 0:
                stick_prompt()
            else:
                fox_prompt()
            decode(l)
            project_out(l)
            with together():
                h_ready = norm(f"ffn{l}", 2 + l)
                ffn(l, h_ready, ffn_parameters(l))
        norm("final", 4, final=True)
        store_y()


_INS = ['x_prompt', 'x_sample', 'cache_k', 'cache_v', 'cache_logf', 'state_conv', 'page_table',
        'norm_mix', 'norm_ffn', 'norm_final', 'w_qkv', 'w_o', 'fox_w_f', 'fox_b_f',
        'ffn_w_a', 'ffn_w_b', 'ffn_conv_w', 'ffn_conv_b', 'ffn_w_down']


def kernel(**inputs):
    import numpy as _np
    import concourse.bacc as _bacc
    from concourse import mybir as _mybir
    from concourse.bass_utils import run_bass_kernel_spmd as _run

    depth, _, _, nkv, dh = inputs['cache_k'].shape
    b, seq, d = inputs['x_prompt'].shape
    nb = inputs['x_sample'].shape[0]
    nh = inputs['cache_logf'].shape[2]
    f = inputs['ffn_w_a'].shape[2]
    outs = [(b, seq, d), (nb, 1, d),
            (depth, b, seq, nkv, dh), (depth, b, seq, nkv, dh), (depth, nb, 1, nkv, dh), (depth, nb, 1, nkv, dh),
            (b, seq, nh), (nb, 1, nh), (depth, b, 2, f), (depth, nb, 2, f)]
    nc = _bacc.Bacc("TRN2", target_bir_lowering=False, num_devices=1)
    arrays, args = {}, []
    for name in _INS:
        a = _np.ascontiguousarray(inputs[name])
        arrays[f"in_{name}_dram"] = a
        args.append(nc.dram_tensor(f"in_{name}_dram", a.shape, _mybir.dt.from_np(a.dtype), kind="ExternalInput").ap())
    for i, shape in enumerate(outs):
        args.append(nc.dram_tensor(f"out_{i}_dram", shape, _mybir.dt.float32, kind="ExternalOutput").ap())
    trunk_program(nc, *args)
    r = _run(nc, [arrays], core_ids=[0])
    got = [r.results[0][f"out_{i}_dram"] for i in range(len(outs))]
    return tuple(got[:8]) + (None, None) + tuple(got[8:])
```
